# Optimizing a Trainium2 kernel written in Bass

```python
import math
import jax, jax.numpy as jnp
from jax import lax
import numpy as np

D_MODEL = 1024
BATCH = 1
SEQ = 512
DEPTH = 2

PLE_DIM = 256
HEAD_DIM = 64
ROPE_THETA = 10000.0
Q_BLOCK = 128
NEG = -1e30
BIG = 1e30
EPS = 1e-6
H_A = 8
W_A = H_A * HEAD_DIM
FORGET_BIAS_MEAN = 4.0
H_B = 8
G_B = 2
W_B = H_B * HEAD_DIM
KV_B = G_B * HEAD_DIM
L_CMP = 32
CMP_STRIDE = 16
CMP_HIDDEN = 256
L_SEL = 64
TOP_N = 16
SEL_Q_BLOCK = 64
WINDOW = 512
H_C = 4
DH_C = HEAD_DIM
W_C = H_C * 2 * DH_C
N_BRANCH = 3
SPLIT_SIZES = (W_A, W_A, W_A, H_A, W_A,
               W_B, KV_B, KV_B, KV_B, KV_B, KV_B, KV_B, 3 * H_B, W_B,
               2 * H_C * DH_C, 2 * H_C * DH_C, W_C, W_C,
               N_BRANCH * D_MODEL)
N_IN = sum(SPLIT_SIZES)

kernel_name = 'hybrid_fox_nsa_diff_gated_merge'

def rmsnorm(x, g):
    xf = x.astype(jnp.float32)
    y = xf * lax.rsqrt(jnp.mean(xf * xf, axis=-1, keepdims=True) + EPS)
    return (y * g.astype(jnp.float32)).astype(x.dtype)

def rope(t, positions):
    half = t.shape[-1] // 2
    inv_freq = ROPE_THETA ** (-jnp.arange(half, dtype=jnp.float32) / half)
    ang = positions.astype(jnp.float32)[:, :, None, None] * inv_freq
    cos, sin = jnp.cos(ang), jnp.sin(ang)
    tf = t.astype(jnp.float32)
    t1, t2 = tf[..., :half], tf[..., half:]
    return jnp.concatenate([t1 * cos - t2 * sin, t2 * cos + t1 * sin], axis=-1).astype(t.dtype)

def split_cols(proj):
    points = np.cumsum(np.array(SPLIT_SIZES))[:-1].tolist()
    return jnp.split(proj, points, axis=-1)

def forgetting_attention(q, k, v, logf):
    B, S, H, Dh = q.shape
    nb = S // Q_BLOCK
    scale = Dh ** -0.5
    c = jnp.cumsum(logf, axis=1)
    c_keys = c.transpose(0, 2, 1)
    q_blocks = q.reshape(B, nb, Q_BLOCK, H, Dh).transpose(1, 0, 2, 3, 4)
    c_blocks = c.reshape(B, nb, Q_BLOCK, H).transpose(1, 0, 3, 2)
    kpos = jnp.arange(S)

    def block(args):
        n, qi, ci = args
        s = jnp.einsum('bqhd,bkhd->bhqk', qi, k, preferred_element_type=jnp.float32) * scale
        s = s + ci[..., None] - c_keys[:, :, None, :]
        qpos = n * Q_BLOCK + jnp.arange(Q_BLOCK)
        mask = kpos[None, :] <= qpos[:, None]
        prob = jax.nn.softmax(jnp.where(mask, s, NEG), axis=-1)
        return jnp.einsum('bhqk,bkhd->bqhd', prob.astype(v.dtype), v)

    out = lax.map(block, (jnp.arange(nb), q_blocks, c_blocks))
    return out.transpose(1, 0, 2, 3, 4).reshape(B, S, H, Dh)

def compress_blocks(t, pe, w1, b1, w2):
    B, S, G, Dh = t.shape
    n_c = (S - L_CMP) // CMP_STRIDE + 1
    idx = jnp.arange(n_c)[:, None] * CMP_STRIDE + jnp.arange(L_CMP)[None, :]
    blocks = t[:, idx] + pe[None, None, :, None, :]
    flat = blocks.transpose(0, 1, 3, 2, 4).reshape(B, n_c, G, L_CMP * Dh)
    hid = jax.nn.silu(flat @ w1 + b1)
    return hid @ w2

def nsa_attention(q, q_rot, k_cmp, v_cmp, k_sel, v_sel, k_win, v_win, gates):
    B, S, H, Dh = q.shape
    G = k_sel.shape[2]
    hpg = H // G
    scale = Dh ** -0.5
    n_c = k_cmp.shape[1]
    n_sel = S // L_SEL
    top_n = min(TOP_N, n_sel)
    t = jnp.arange(S)

    qg = q.reshape(B, S, G, hpg, Dh)
    s_c = jnp.einsum('bsghd,bcgd->bghsc', qg, k_cmp, preferred_element_type=jnp.float32) * scale
    c_end = jnp.arange(n_c) * CMP_STRIDE + L_CMP - 1
    mask_c = c_end[None, :] <= t[:, None]
    p_c = jax.nn.softmax(jnp.where(mask_c, s_c, NEG), axis=-1) * mask_c
    o_cmp = jnp.einsum('bghsc,bcgd->bsghd', p_c.astype(v_cmp.dtype), v_cmp).reshape(B, S, H, Dh)

    c_start = jnp.arange(n_c) * CMP_STRIDE
    j_start = jnp.arange(n_sel) * L_SEL
    cover = ((c_start[:, None] < j_start[None, :] + L_SEL)
             & (c_start[:, None] + L_CMP > j_start[None, :])).astype(jnp.float32)
    imp = jnp.einsum('bghsc,cj->bgsj', p_c, cover)
    jj = jnp.arange(n_sel)[None, :]
    tb = (t // L_SEL)[:, None]
    valid = jj <= tb
    forced = (jj == 0) | (jj == tb) | (jj == tb - 1)
    score = jnp.where(forced, BIG, jnp.where(valid, imp, -BIG))
    _, sel_idx = lax.top_k(score, top_n)

    ks_blk = k_sel.reshape(B, n_sel, L_SEL, G, Dh).transpose(0, 3, 1, 2, 4)
    vs_blk = v_sel.reshape(B, n_sel, L_SEL, G, Dh).transpose(0, 3, 1, 2, 4)
    nqb = S // SEL_Q_BLOCK
    q_sb = q_rot.reshape(B, nqb, SEL_Q_BLOCK, G, hpg, Dh).transpose(1, 0, 3, 2, 4, 5)
    idx_sb = sel_idx.reshape(B, G, nqb, SEL_Q_BLOCK, top_n).transpose(2, 0, 1, 3, 4)
    bi = jnp.arange(B)[:, None, None, None]
    gi = jnp.arange(G)[None, :, None, None]

    def sel_block(args):
        n, qi, ii = args
        kg = ks_blk[bi, gi, ii]
        vg = vs_blk[bi, gi, ii]
        s = jnp.einsum('bgqhd,bgqnld->bghqnl', qi, kg, preferred_element_type=jnp.float32) * scale
        kpos = ii[..., None] * L_SEL + jnp.arange(L_SEL)
        qpos = n * SEL_Q_BLOCK + jnp.arange(SEL_Q_BLOCK)
        mask = kpos <= qpos[None, None, :, None, None]
        s = jnp.where(mask[:, :, None], s, NEG).reshape(B, G, hpg, SEL_Q_BLOCK, top_n * L_SEL)
        prob = jax.nn.softmax(s, axis=-1).reshape(B, G, hpg, SEL_Q_BLOCK, top_n, L_SEL)
        return jnp.einsum('bghqnl,bgqnld->bqghd', prob.astype(vg.dtype), vg)

    o_sel = lax.map(sel_block, (jnp.arange(nqb), q_sb, idx_sb))
    o_sel = o_sel.transpose(1, 0, 2, 3, 4, 5).reshape(B, S, H, Dh)

    kw_pad = jnp.pad(k_win, ((0, 0), (WINDOW, 0), (0, 0), (0, 0)))
    vw_pad = jnp.pad(v_win, ((0, 0), (WINDOW, 0), (0, 0), (0, 0)))
    nwb = S // Q_BLOCK
    q_wb = q_rot.reshape(B, nwb, Q_BLOCK, G, hpg, Dh).transpose(1, 0, 2, 3, 4, 5)
    ii_ = jnp.arange(Q_BLOCK)[:, None]
    jw = jnp.arange(Q_BLOCK + WINDOW)[None, :]
    band = (jw > ii_) & (jw <= ii_ + WINDOW)

    def win_block(args):
        n, qi = args
        kk = lax.dynamic_slice_in_dim(kw_pad, n * Q_BLOCK, Q_BLOCK + WINDOW, axis=1)
        vv = lax.dynamic_slice_in_dim(vw_pad, n * Q_BLOCK, Q_BLOCK + WINDOW, axis=1)
        s = jnp.einsum('bqghd,bkgd->bghqk', qi, kk, preferred_element_type=jnp.float32) * scale
        mask = band & (n * Q_BLOCK + jw - WINDOW >= 0)
        prob = jax.nn.softmax(jnp.where(mask, s, NEG), axis=-1)
        return jnp.einsum('bghqk,bkgd->bqghd', prob.astype(vv.dtype), vv)

    o_win = lax.map(win_block, (jnp.arange(nwb), q_wb))
    o_win = o_win.transpose(1, 0, 2, 3, 4, 5).reshape(B, S, H, Dh)

    return gates[..., 0:1] * o_cmp + gates[..., 1:2] * o_sel + gates[..., 2:3] * o_win

def differential_attention(q, k, v, lam, lam_init, subln_g):
    B, S, H, _, Dh = q.shape
    nb = S // Q_BLOCK
    scale = Dh ** -0.5
    q_blocks = q.reshape(B, nb, Q_BLOCK, H, 2, Dh).transpose(1, 0, 2, 3, 4, 5)
    kpos = jnp.arange(S)

    def block(args):
        n, qi = args
        s = jnp.einsum('bqhmd,bkhmd->bhmqk', qi, k, preferred_element_type=jnp.float32) * scale
        qpos = n * Q_BLOCK + jnp.arange(Q_BLOCK)
        mask = kpos[None, :] <= qpos[:, None]
        prob = jax.nn.softmax(jnp.where(mask, s, NEG), axis=-1)
        w = prob[:, :, 0] - lam * prob[:, :, 1]
        return jnp.einsum('bhqk,bkhe->bqhe', w.astype(v.dtype), v)

    out = lax.map(block, (jnp.arange(nb), q_blocks))
    out = out.transpose(1, 0, 2, 3, 4).reshape(B, S, H, 2 * Dh)
    return rmsnorm(out, subln_g) * (1.0 - lam_init)

def setup_inputs(seed: int = 0) -> dict:
    key = jax.random.key(seed)
    ks = jax.random.split(key, 24)
    f32 = jnp.float32

    def nrm(k, shape, scale):
        return jax.random.normal(k, shape, f32) * scale

    x = nrm(ks[0], (BATCH, SEQ, D_MODEL), 1.0)
    p = nrm(ks[1], (DEPTH, BATCH, SEQ, PLE_DIM), 1.0)
    offset = jax.random.randint(ks[2], (BATCH, 1), 0, 1024, dtype=jnp.int32)
    positions = offset + jnp.arange(SEQ, dtype=jnp.int32)[None, :]
    return {
        'x': x,
        'p': p,
        'positions': positions,
        'norm_g': 1.0 + nrm(ks[3], (DEPTH, D_MODEL), 0.02),
        'w_in': nrm(ks[4], (DEPTH, D_MODEL, N_IN), D_MODEL ** -0.5),
        'b_forget': FORGET_BIAS_MEAN + nrm(ks[5], (DEPTH, H_A), 0.5),
        'cmp_pe_k': nrm(ks[6], (DEPTH, L_CMP, HEAD_DIM), 0.1),
        'cmp_w1_k': nrm(ks[7], (DEPTH, L_CMP * HEAD_DIM, CMP_HIDDEN), (L_CMP * HEAD_DIM) ** -0.5),
        'cmp_b1_k': nrm(ks[8], (DEPTH, CMP_HIDDEN), 0.01),
        'cmp_w2_k': nrm(ks[9], (DEPTH, CMP_HIDDEN, HEAD_DIM), CMP_HIDDEN ** -0.5),
        'cmp_pe_v': nrm(ks[10], (DEPTH, L_CMP, HEAD_DIM), 0.1),
        'cmp_w1_v': nrm(ks[11], (DEPTH, L_CMP * HEAD_DIM, CMP_HIDDEN), (L_CMP * HEAD_DIM) ** -0.5),
        'cmp_b1_v': nrm(ks[12], (DEPTH, CMP_HIDDEN), 0.01),
        'cmp_w2_v': nrm(ks[13], (DEPTH, CMP_HIDDEN, HEAD_DIM), CMP_HIDDEN ** -0.5),
        'diff_lam': nrm(ks[14], (DEPTH, 4, DH_C), 0.1),
        'diff_subln_g': 1.0 + nrm(ks[15], (DEPTH, 2 * DH_C), 0.02),
        'w_br_a': nrm(ks[16], (DEPTH, W_A, D_MODEL), W_A ** -0.5),
        'w_br_b': nrm(ks[17], (DEPTH, W_B, D_MODEL), W_B ** -0.5),
        'w_br_c': nrm(ks[18], (DEPTH, W_C, D_MODEL), W_C ** -0.5),
        'w_out': nrm(ks[19], (DEPTH, D_MODEL, D_MODEL), D_MODEL ** -0.5),
        'w_ple': nrm(ks[20], (DEPTH, PLE_DIM, D_MODEL), PLE_DIM ** -0.5),
        'w_ple_gate': nrm(ks[21], (DEPTH, D_MODEL, D_MODEL), D_MODEL ** -0.5),
        'final_g': 1.0 + nrm(ks[22], (D_MODEL,), 0.02),
    }

def reference(x, p, positions, norm_g, w_in, b_forget, cmp_pe_k, cmp_w1_k, cmp_b1_k, cmp_w2_k,
              cmp_pe_v, cmp_w1_v, cmp_b1_v, cmp_w2_v, diff_lam, diff_subln_g,
              w_br_a, w_br_b, w_br_c, w_out, w_ple, w_ple_gate, final_g):
    B, S, D = x.shape
    for i in range(DEPTH):
        h = rmsnorm(x, norm_g[i])
        proj = jnp.einsum('bsd,dn->bsn', h, w_in[i])
        (qa, ka, va, fa, za,
         qb, kcb, vcb, ksb, vsb, kwb, vwb, gb, zb,
         qc, kc, vc, zc, mg) = split_cols(proj)

        logf = jax.nn.log_sigmoid(fa.astype(jnp.float32) + b_forget[i].astype(jnp.float32))
        ya = forgetting_attention(qa.reshape(B, S, H_A, HEAD_DIM), ka.reshape(B, S, H_A, HEAD_DIM),
                                  va.reshape(B, S, H_A, HEAD_DIM), logf)
        ya = ya.reshape(B, S, W_A) * jax.nn.silu(za)

        qb = qb.reshape(B, S, H_B, HEAD_DIM)
        qb_rot = rope(qb, positions)
        k_cmp = compress_blocks(kcb.reshape(B, S, G_B, HEAD_DIM), cmp_pe_k[i], cmp_w1_k[i], cmp_b1_k[i], cmp_w2_k[i])
        v_cmp = compress_blocks(vcb.reshape(B, S, G_B, HEAD_DIM), cmp_pe_v[i], cmp_w1_v[i], cmp_b1_v[i], cmp_w2_v[i])
        k_sel = rope(ksb.reshape(B, S, G_B, HEAD_DIM), positions)
        k_win = rope(kwb.reshape(B, S, G_B, HEAD_DIM), positions)
        gates = jax.nn.sigmoid(gb.reshape(B, S, H_B, 3))
        yb = nsa_attention(qb, qb_rot, k_cmp, v_cmp, k_sel, vsb.reshape(B, S, G_B, HEAD_DIM),
                           k_win, vwb.reshape(B, S, G_B, HEAD_DIM), gates)
        yb = yb.reshape(B, S, W_B) * jax.nn.silu(zb)

        qc = rope(qc.reshape(B, S, 2 * H_C, DH_C), positions).reshape(B, S, H_C, 2, DH_C)
        kc = rope(kc.reshape(B, S, 2 * H_C, DH_C), positions).reshape(B, S, H_C, 2, DH_C)
        lam_init = 0.8 - 0.6 * math.exp(-0.3 * i)
        lq1, lk1, lq2, lk2 = diff_lam[i].astype(jnp.float32)
        lam = jnp.exp(jnp.sum(lq1 * lk1)) - jnp.exp(jnp.sum(lq2 * lk2)) + lam_init
        yc = differential_attention(qc, kc, vc.reshape(B, S, H_C, 2 * DH_C), lam, lam_init, diff_subln_g[i])
        yc = yc.reshape(B, S, W_C) * jax.nn.silu(zc)

        g = jax.nn.sigmoid(mg).reshape(B, S, N_BRANCH, D)
        merged = (g[:, :, 0] * (ya @ w_br_a[i]) + g[:, :, 1] * (yb @ w_br_b[i])
                  + g[:, :, 2] * (yc @ w_br_c[i]))
        x = x + merged @ w_out[i]

        x = x + jax.nn.sigmoid(x @ w_ple_gate[i]) * (p[i] @ w_ple[i])
    return rmsnorm(x, final_g)


_drawn_inputs = setup_inputs


def setup_inputs(seed=0):
    import zlib

    import numpy as np

    out = dict(_drawn_inputs(seed))
    spreads = {}
    factors = {'norm_g': 4.647,
     'b_forget': 2.827,
     'cmp_pe_k': 8.0,
     'cmp_w1_k': 3.285,
     'cmp_b1_k': 8.0,
     'cmp_w2_k': 3.374,
     'cmp_pe_v': 4.86,
     'cmp_b1_v': 23.221,
     'diff_subln_g': 8.0,
     'final_g': 7.97}
    for name, (base, spread) in spreads.items():
        noise = np.random.default_rng([zlib.crc32(name.encode()), seed]).standard_normal(out[name].shape)
        drawn = base * np.exp(spread * noise) if base else spread * noise
        out[name] = __import__('jax').numpy.asarray(drawn.astype(out[name].dtype))
    for name, factor in factors.items():
        out[name] = (out[name] * factor).astype(out[name].dtype)
    return out
```

```python
from contextlib import ExitStack

import numpy as np

import concourse.bass as bass
from concourse import mybir

ALU = mybir.AluOpType
ACT = mybir.ActivationFunctionType
AX = mybir.AxisListType
F32 = mybir.dt.float32
F32R = mybir.dt.float32r
BF16 = mybir.dt.bfloat16
I32 = mybir.dt.int32

P = 128
HD = 64
EPS = 1e-6
NEG = -1e30
ROPE_THETA = 10000.0

W_MIX = 512
COL = {}
_at = 0
for _name, _n in (("qa", 512), ("ka", 512), ("va", 512), ("fa", 8), ("za", 512),
                  ("qb", 512), ("kcb", 128), ("vcb", 128), ("ksb", 128), ("vsb", 128), ("kwb", 128), ("vwb", 128),
                  ("gb", 24), ("zb", 512), ("qc", 512), ("kc", 512), ("vc", 512), ("zc", 512), ("mg", 3072)):
    COL[_name] = _at
    _at += _n

RAW = 4
SPL = 2
NP_ = 4
UNITS = 12


def y_slot(u):
    return 0 if u < 4 else u % 4


def branch(u):
    return "ABC"[u // 4]



def dense_tiles():
    st = {-1: [("fg", 0)] + [("va", j) for j in range(4)] + [("qa", 0), ("ka", 0)]}
    st[0] = [("qa", 1), ("ka", 1), ("za", 0), ("kcb", 0)]
    st[1] = [("qa", 2), ("ka", 2), ("w1k", 0), ("za", 1), ("w1k", 1), ("ksb", 0)]
    st[2] = [("qa", 3), ("ka", 3), ("w1k", 2), ("za", 2), ("w1k", 3), ("vcb", 0), ("kwb", 0)]
    st[3] = [("qb", 0), ("w1v", 0), ("za", 3), ("w1v", 1), ("w1v", 2), ("vsb", 0), ("w1v", 3), ("vwb", 0)]
    st[4] = [("qb", 1), ("vc", 0), ("zb", 0), ("mga", 0), ("bra", 0), ("mga", 1), ("bra", 1)]
    st[5] = [("qb", 2), ("vc", 1), ("zb", 1), ("mga", 2), ("bra", 2), ("mga", 3), ("bra", 3)]
    st[6] = [("qb", 3), ("vc", 2), ("zb", 2), ("vc", 3), ("mga", 4), ("bra", 4), ("mga", 5), ("bra", 5)]
    st[7] = [("qc", 0), ("kc", 0), ("zb", 3), ("mga", 6), ("bra", 6), ("mga", 7), ("bra", 7)]
    st[8] = [("qc", 1), ("kc", 1), ("mgb", 0), ("zc", 0), ("brb", 0), ("mgb", 1), ("brb", 1)]
    st[9] = [("qc", 2), ("kc", 2), ("mgb", 2), ("zc", 1), ("brb", 2), ("mgb", 3), ("brb", 3)]
    st[10] = [("qc", 3), ("kc", 3), ("mgb", 4), ("zc", 2), ("brb", 4), ("mgb", 5), ("brb", 5)]
    st[11] = [("mgb", 6), ("brb", 6), ("zc", 3), ("mgb", 7), ("brb", 7)]
    return st


KT = {"bra": 4, "brb": 4, "brc": 4, "ple": 2}
ROTATED = ("qb", "ksb", "kwb", "qc", "kc")
VALUES = ("va", "vsb", "vwb", "vc")
ACT_EVAC = ("qa", "ka", "za", "zb", "zc", "fg") + ROTATED + VALUES + ("mga", "mgb", "mgc", "gate")
DVE_EVAC = ("qa", "ka", "za", "zb", "zc", "fg", "kcb", "vcb", "w1k", "w1v", "bra", "brb", "brc", "out", "ple")


def kt(kind):
    return KT.get(kind, 8)


class Count:

    def __init__(self):
        self.order = {}

    def add(self, key):
        assert key not in self.order, key
        self.order[key] = len(self.order) + 1

    def after(self, key):
        return self.order[key]

    def __len__(self):
        return len(self.order)


def make_schedule(NQ):
    stages = dense_tiles()
    tiles = []
    for s in sorted(stages):
        tiles += [(kind, n, s) for kind, n in stages[s]]
    first = {}
    for t, (kind, n, s) in enumerate(tiles):
        first.setdefault(s, t)

    rows, prob_rows = [], []
    for u in range(UNITS):
        for i in range(NQ):
            if branch(u) == "A":
                maps = [("a", 0), ("a", 1)]
            elif branch(u) == "B":
                maps = [("sel", 0), ("sel", 1), ("win", 0), ("win", 1)]
            else:
                maps = [("c", 0), ("c", 1)]
            r0 = len(rows)
            rows += [(u, i, m, h) for m, h in maps]
            if branch(u) == "C":
                prob_rows.append((u, i, "c", 0, r0 + 1, True))
            else:
                for j, (m, h) in enumerate(maps):
                    prob_rows.append((u, i, m, h, r0 + j, j == len(maps) - 1))

    items = []
    follow = []

    def step_follow():
        for f in follow:
            f[0] -= 1
        while follow and follow[0][0] <= 0:
            items.append(follow.pop(0)[1])

    def dense_groups(s):
        for t in [t for t, x in enumerate(tiles) if x[2] == s]:
            for k in range(kt(tiles[t][0])):
                yield t, k

    def emit_group(g):
        t, k = g
        items.append(("mm", t, k))
        kind = tiles[t][0]
        step_follow()
        if k == kt(kind) - 1:
            items.append(("end", t))
            if kind in ROTATED:
                follow.append([7, ("rot", t)])
            if kind in VALUES:
                follow.append([2, ("vt", t)])
            if kind == "fg":
                follow.append([3, ("gates", t)])
            if kind == "w1k" and tiles[t][1] == 3:
                follow.append([5, ("kcmp", t)])
            if kind == "w1v" and tiles[t][1] == 3:
                follow.append([5, ("vcmp", t)])
            follow.sort(key=lambda f: f[0])

    for g in dense_groups(-1):
        emit_group(g)

    vq, late, combs = [], [], []
    tick = 0
    ti = 0
    for s in range(UNITS):
        groups = list(dense_groups(s))
        rs = [r for r, x in enumerate(rows) if x[0] == s]
        tail = 6 if s == UNITS - 1 else 0
        N = len(rs) + tail
        G = len(groups)
        done = 0
        for j in range(N):
            parts = []
            if j < len(rs):
                r = rs[j]
                parts.append(("S", r))
            if j < len(rs) and branch(s) == "B" and j < 3:
                parts.append((("cs", "cx", "ct")[j], s))
            while combs and combs[0][0] <= tick:
                parts.append(combs.pop(0)[1])
            if j < len(rs) and branch(s) == "C" and rows[rs[j]][3] == 1:
                combs.append((tick + 1, ("CB", rs[j])))
            if ti < len(prob_rows):
                lag = 2 if branch(prob_rows[ti][0]) == "C" else 1
                limit = tick - lag
                while ti < len(prob_rows) and prob_rows[ti][4] <= limit:
                    parts.append(("T", ti))
                    vq.append((tick + 1, ti))
                    ti += 1
            while late and late[0][0] <= tick:
                parts.append(late.pop(0)[1])
            while vq and vq[0][0] <= tick:
                k = vq.pop(0)[1]
                parts.append(("V", k))
                if prob_rows[k][5]:
                    u, i = prob_rows[k][:2]
                    parts.append(("N", NQ * u + i))
                    if i == NQ - 1:
                        if branch(u) == "C":
                            late += [(tick + 1, ("MS", u)), (tick + 2, ("Y", u))]
                        else:
                            late.append((tick + 1, ("Y", u)))
            if s == 8 and j == 4:
                parts += [("YS", u) for u in range(4, 8)]
            want = (j + 1) * G // N
            n = want - done
            for m, part in enumerate(parts):
                items.append(part)
                if part[0] == "Y" and branch(part[1]) == "A":
                    items.append(("YS", part[1]))
                share = (m + 1) * n // len(parts) - m * n // len(parts)
                if m == len(parts) - 1:
                    share = want - done
                for _ in range(share):
                    emit_group(groups[done])
                    done += 1
            if not parts:
                while done < want:
                    emit_group(groups[done])
                    done += 1
            tick += 1
    while follow:
        items.append(follow.pop(0)[1])
    items += [("YS", u) for u in range(8, 12)]
    assert not late and not vq and ti == len(prob_rows)
    where = {x: n for n, x in enumerate(items)}
    for u in range(1, UNITS):
        z = tiles.index(("z" + branch(u).lower(), u % 4, u))
        assert where[("end", z)] > where[("Y", u - 1)], u
        assert where[("end", z)] < where[("Y", u)], u
        assert where[("Y", u - 1)] < where[("N", NQ * u)], u
    return tiles, rows, prob_rows, items


def hybrid_trunk(nc, x, p, positions, norm_g, w_in, b_forget, cmp_pe_k, cmp_w1_k, cmp_b1_k, cmp_w2_k,
                 cmp_pe_v, cmp_w1_v, cmp_b1_v, cmp_w2_v, diff_lam, diff_subln_g,
                 w_br_a, w_br_b, w_br_c, w_out, w_ple, w_ple_gate, final_g, rope_consts, layer_consts, out):
    _, S, D = x.shape
    DEPTH = norm_g.shape[0]
    NQ = S // P
    NM = D // P
    CS, NC = 16, (S - 32) // 16 + 1
    C32 = 32
    QSCALE = HD ** -0.5

    tiles, rows, prob_rows, items = make_schedule(NQ)
    T0 = len(tiles)
    T1 = T0 + 2 * NM
    T2 = T1 + NM
    T3 = T2 + 2 * NM
    assert NM % 4 == 0

    act_evac, dve_evac, rots, qk_ready, misc = Count(), Count(), Count(), Count(), Count()
    pt_act, pt_dve, ysplit, hids = Count(), Count(), Count(), Count()
    for it in items:
        if it[0] == "end":
            kind, n, _ = tiles[it[1]]
            if kind in ACT_EVAC:
                act_evac.add(it[1])
            if kind in DVE_EVAC:
                dve_evac.add(it[1])
            if kind in ROTATED:
                rots.add(it[1])
            if kind in ("w1k", "w1v") and n % 2:
                hids.add((kind, n))
        elif it[0] == "rot":
            qk_ready.add(tiles[it[1]][:2])
        elif it[0] in ("vt", "gates", "kcmp", "vcmp", "cs", "ct", "Y"):
            misc.add(it)
        elif it[0] == "T":
            (pt_act if it[1] % 2 and branch(prob_rows[it[1]][0]) == "B" else pt_dve).add(it[1])
        elif it[0] == "YS":
            ysplit.add(it[1])
    DA0 = NM
    rows_before = {}
    for r, x_ in enumerate(rows):
        rows_before.setdefault(x_[0], r)
    th_slot, n_th = {}, 0
    for t, (kind, n, _) in enumerate(tiles):
        if kind in ("fg", "za", "zb", "zc", "mga", "mgb"):
            th_slot[t] = n_th % 2
            n_th += 1
    AE0, DE0 = len(act_evac), len(dve_evac)
    AE1, DE1 = AE0 + NM, DE0 + NM
    DE2 = DE1 + NM

    prob_of_row = {}
    for k, x_ in enumerate(prob_rows):
        prob_of_row[x_[4]] = k
        if x_[2] == "c":
            prob_of_row[x_[4] - 1] = k
    first_prob, last_prob = {}, {}
    for k, (u, i, *_r) in enumerate(prob_rows):
        first_prob.setdefault((u, i), k)
        last_prob[(u, i)] = k

    def w_cols(L, w, c0, n, k):
        return w[bass.ds(L, 1), 0:k * P, bass.ds(c0, n)].rearrange("a (k p) n -> p (a k) n", p=P)

    def sources(L, kind, n):
        full = lambda w, c0: [(slice(0, P), slice(0, P), w_cols(L, w, c0, P, kt(kind)))]
        if kind == "fg":
            return [(slice(0, P), slice(0, 32), w_cols(L, w_in, COL["fa"], 32, 8)),
                    (slice(0, P), slice(32, P), w_cols(L, w_in, COL["gb"], 96, 8))]
        if kind in ("qb", "zb"):
            return [(slice(0, P), slice(HD * g, HD * g + HD), w_cols(L, w_in, COL[kind] + 256 * g + HD * n, HD, 8))
                    for g in range(2)]
        if kind in ("w1k", "w1v"):
            w = cmp_w1_k if kind == "w1k" else cmp_w1_v
            ht, half = n // 2, n % 2
            src = w[bass.ds(L, 1), half * 1024:(half + 1) * 1024, ht * P:(ht + 1) * P]
            return [(slice(0, P), slice(0, P), src.rearrange("a (k p) n -> p (a k) n", p=P))]
        if kind in ("mga", "mgb", "mgc"):
            return full(w_in, COL["mg"] + D * "abc".index(kind[2]) + n * P)
        if kind == "brb":
            return [(slice(HD * g, HD * g + HD), slice(0, P),
                     w_br_b[bass.ds(L, 1), 256 * g:256 * g + 256, bass.ds(n * P, P)].rearrange(
                         "a (k p) n -> p (a k) n", p=HD)) for g in range(2)]
        if kind in ("bra", "brc"):
            return full(w_br_a if kind == "bra" else w_br_c, n * P)
        if kind == "out":
            return full(w_out, n * P)
        if kind == "gate":
            return full(w_ple_gate, n * P)
        if kind == "ple":
            return full(w_ple, n * P)
        return full(w_in, COL[kind] + n * P)

    landed, slot_sum = [], [0] * RAW
    for t, (kind, n, _) in enumerate(tiles):
        slot_sum[t % RAW] += 16 * (2 if kind in ("fg", "qb", "zb", "brb") else 1)
        landed.append(slot_sum[t % RAW])

    ctx = ExitStack()
    with ctx:
        def sb(name, shape, dt=F32):
            return ctx.enter_context(nc.sbuf_tensor(name, shape, dt))

        def bank(name):
            return ctx.enter_context(nc.psum_tensor(name, [P, 512], F32))

        sems = []

        def sem(name):
            s = ctx.enter_context(nc.semaphore(name))
            sems.append(s)
            return s

        xT = sb("xT", [P, NM, S])
        acc = sb("acc", [P, NM, S])
        h_hi = sb("h_hi", [P, NM, S], F32R)
        h_lo = sb("h_lo", [P, NM, S], F32R)
        raw = sb("raw", [P, RAW, 8 * P])
        w_hi = sb("w_hi", [P, SPL, 8 * P], F32R)
        w_lo = sb("w_lo", [P, SPL, 8 * P], F32R)
        arena = sb("arena", [P, 16 * S], F32R)

        def part(n, k=1):
            return arena[:, n * S:(n + k) * S]
        q_hi, q_lo = [part(0), part(1)], [part(2), part(3)]
        k_hi, k_lo = [part(4), part(5)], [part(6), part(7)]
        ks_hi, ks_lo, kw_hi, kw_lo = part(8), part(9), part(10), part(11)
        flat_hi = part(12, 2).rearrange("p (m c) -> p m c", m=16)
        flat_lo = part(14, 2).rearrange("p (m c) -> p m c", m=16)
        x1_hi = part(0, NM).rearrange("p (m s) -> p m s", m=NM)
        x1_lo = part(NM, NM).rearrange("p (m s) -> p m s", m=NM)
        y_hi = sb("y_hi", [P, 4, S], F32R)
        y_lo = sb("y_lo", [P, 4, S], F32R)
        y_f = sb("y_f", [P, 4, S])
        v_ac = sb("v_ac", [P, NQ, 512])
        v_b = sb("v_b", [P, NQ, 256])
        probs = sb("probs", [P, NP_, S])
        pT = sb("pT", [P, 2, S])
        zs = sb("zs", [P, S])
        th = sb("th", [P, 2, S])
        vT = y_f[:, 3, :]
        qf = sb("qf", [P, S])
        rx = sb("rx", [P, S])
        rs = sb("rs", [P, S])
        rb = sb("rb", [P, S])
        rc = sb("rc", [P, S])
        flat = v_b[:].rearrange("p i c -> p (i c)").rearrange("p (m c) -> p m c", m=16)
        cosT = sb("cosT", [P, S])
        sinT = sb("sinT", [P, S])
        ssum = zs
        ident = sb("ident", [P, P])
        ones = sb("ones", [P, P])
        identb = sb("identb", [P, P], BF16)
        maskb = sb("maskb", [P, P], BF16)
        cmask = sb("cmask", [P, NQ, C32])
        self_ = sb("self_", [P, 8])
        selr = sb("selr", [P, 8], F32R)
        ck = sb("ck", [P, S], F32R)
        par = sb("par", [P, 48])
        finp = sb("finp", [P, 8])
        w2k = y_f[:, 1, 128:384].rearrange("p (a c) -> p a c", a=2)
        w2v = y_f[:, 1, 384:512].rearrange("p (a c) -> p a c", a=2)
        bfor = sb("bfor", [8, 1])
        lconst = sb("lconst", [P, 2])
        rconst = sb("rconst", [P, 2])
        lams = sb("lams", [P, 8])
        gsc = sb("gsc", [P, 1])
        gates = sb("gates", [P, NQ, 24])
        lf = probs[0:8]
        hacc = y_f[:, 1, 0:128].rearrange("p (a c) -> p a c", a=2)
        hid = y_f[:, 2, :].rearrange("p (a g b c) -> p a g b c", a=2, g=2, b=4)
        kcmpT = sb("kcmpT", [P, 2 * C32])
        vbd = sb("vbd", [P, P])
        cs_ = sb("cs_", [P, NQ, 2, C32])
        pc = cs_
        pcT = sb("pcT", [P, 2, P])
        cmx = sb("cmx", [P, 2 * NQ])
        nmax = sb("nmax", [P, 8])
        sums = sb("sums", [P, 2, NQ, 6])
        coef = sb("coef", [P, 2, 8])
        y_q = sb("y_q", [P, NQ, P])
        prow = y_q[0:48, 0, :]
        tmp = sb("tmp", [P, 384])
        msq = sb("msq", [P, 4, NQ])
        halfs = sb("halfs", [P, NQ])
        sqj = cs_[:].rearrange("p i h c -> p (i h c)")[:, 0:P]
        lamr = tmp[:, 0:4 * HD]
        hth = cs_[:].rearrange("p i h c -> p (i h c)")[:, P:P + 64]
        rt = qf
        posi = pT[:, 0, :].bitcast(I32)

        Dn = [bank("D0"), bank("D1")]
        Sc = [bank("S0"), bank("S1")]
        Tr = [bank("T0"), bank("T1")]
        Ob = bank("Ob")
        Mb = bank("Mb")

        def f(ap):
            return ap.bitcast(F32)

        i_ld, i_const, i_pe, i_dve, i_act = (sem(n) for n in ("i_ld", "i_const", "i_pe", "i_dve", "i_act"))
        i_fin, i_x = sem("i_fin"), sem("i_x")
        x_tok = acc[:].rearrange("p m s -> p (m s)").rearrange("p (t d) -> p t d", t=NQ)
        with nc.Block() as block:
            @block.sync
            def _(sp):
                sp.dma_start(x_tok, x.rearrange("a (t p) d -> p (a t) d", p=P)).then_inc(i_x, 16)
                sp.dma_start(posi, positions.to_broadcast([P, S])).then_inc(i_ld, 16)
                sp.dma_start(rconst[:], rope_consts).then_inc(i_ld, 16)
                sp.dma_start(prow[0:NM, :], final_g.rearrange("(m p) -> m p", p=P)).then_inc(i_fin, 16)

            @block.gpsimd
            def _(pool):
                pool.memset(ident[:], 0.0).then_inc(i_const, 1)
                pool.wait_ge(i_const, 1)
                pool.affine_select(out=ident[:], in_=ident[:], compare_op=ALU.not_equal, fill=1.0, base=0,
                                   pattern=[[-1, P]], channel_multiplier=1).then_inc(i_const, 1)
                pool.memset(ones[:], 1.0).then_inc(i_const, 1)
                pool.memset(maskb[:], 0.0).then_inc(i_const, 1)
                pool.memset(cmask[:], 0.0).then_inc(i_const, 1)
                pool.memset(self_[:], 0.0).then_inc(i_const, 1)
                pool.memset(halfs[:], -0.5).then_inc(i_const, 1)
                pool.memset(vbd[:], 0.0).then_inc(i_const, 1)
                pool.memset(kcmpT[:], 0.0).then_inc(i_const, 1)
                pool.memset(f(ck[:]), 0.0).then_inc(i_const, 1)
                pool.wait_ge(i_const, 10)
                pool.tensor_copy(identb[:], ident[:]).then_inc(i_const, 1)
                pool.affine_select(out=maskb[:], in_=maskb[:], compare_op=ALU.is_ge, fill=NEG, base=0,
                                   pattern=[[-1, P]], channel_multiplier=1).then_inc(i_const, 1)
                pool.affine_select(out=cmask[:], in_=cmask[:], compare_op=ALU.is_ge, fill=NEG, base=-31,
                                   pattern=[[P, NQ], [-CS, C32]], channel_multiplier=1).then_inc(i_const, 1)
                for n, r in enumerate((0, 32)):
                    pool.affine_select(out=self_[:], in_=self_[:], compare_op=ALU.not_equal, fill=1.0, base=-r,
                                       pattern=[[-1, 8]], channel_multiplier=1).then_inc(i_const, 1)
                    pool.wait_ge(i_const, 14 + n)
                pool.tensor_copy(selr[:], self_[:]).then_inc(i_const, 1)

            NB = NM

            @block.tensor
            def _(pe):
                pe.wait_ge(i_const, 2)
                pe.wait_ge(i_x, 16)
                for m in range(NB):
                    if m >= 2:
                        pe.wait_ge(i_dve, m - 1)
                    for t in range(NQ):
                        ins = pe.transpose(Dn[m % 2][:, t * P:(t + 1) * P], x_tok[:, t, m * P:(m + 1) * P], ident[:])
                    ins.then_inc(i_pe, 1)
                pe.wait_ge(i_fin, 16)
                pe.transpose(Mb[:, 0:NM], prow[0:NM, :], ident[0:NM, 0:NM]).then_inc(i_pe, 1)

            @block.vector
            def _(dve):
                for m in range(NB):
                    dve.wait_ge(i_pe, m + 1)
                    dve.tensor_copy(xT[:, m, :], Dn[m % 2][:]).then_inc(i_dve, 1)
                dve.wait_ge(i_pe, NB + 1)
                dve.tensor_copy(finp[:], Mb[:, 0:NM]).then_inc(i_dve, 1)
                n = NB + 1

                def link(ins):
                    nonlocal n
                    n += 1
                    ins.then_inc(i_dve, 1)
                    dve.wait_ge(i_dve, n)
                for m in range(NM):
                    dve.wait_ge(i_act, m + 1)
                    if m == 0:
                        link(dve.tensor_copy(ssum[:], acc[:, 0, :]))
                    else:
                        link(dve.tensor_tensor(ssum[:], ssum[:], acc[:, m, :], ALU.add))
                dve.wait_ge(i_ld, 32)
                link(dve.tensor_copy(rx[:], posi))
                link(dve.tensor_scalar(rx[:], rx[:], rconst[:, 0:1], None, ALU.mult))
                MAGIC = 12582912.0
                link(dve.tensor_scalar(rs[:], rx[:], 1.0 / (2 * np.pi), MAGIC, ALU.mult, ALU.add))
                link(dve.tensor_scalar(rs[:], rs[:], MAGIC, None, ALU.subtract))
                c1 = 6.28125
                c2 = float(np.float32(np.round((2 * np.pi - c1) * 2 ** 20) / 2 ** 20))
                c3 = 2 * np.pi - c1 - c2
                for c in (c1, c2, c3):
                    link(dve.scalar_tensor_tensor(rx[:], rs[:], -c, rx[:], ALU.mult, ALU.add))
                link(dve.tensor_scalar(rx[:], rx[:], -3.1415925, 3.1415925, ALU.max, ALU.min))
                link(dve.tensor_scalar(rb[:], rx[:], -1.0, None, ALU.mult))
                link(dve.tensor_tensor(rb[:], rb[:], rx[:], ALU.max))
                link(dve.tensor_scalar(rb[:], rb[:], -1.0, float(np.pi / 2), ALU.mult, ALU.add))
                dve.wait_ge(i_act, NM + 2)
                link(dve.tensor_scalar(sinT[:], rc[:], rconst[:, 1:2], None, ALU.mult))

            @block.scalar
            def _(act):
                for m in range(NM):
                    if m == 0:
                        act.wait_ge(i_pe, NB)
                    act.wait_ge(i_dve, m + 1)
                    act.activation(acc[:, m, :], xT[:, m, :], ACT.Square).then_inc(i_act, 1)
                act.wait_ge(i_dve, NB + 1 + NM + 11)
                act.activation(cosT[:], rb[:], ACT.Sin).then_inc(i_act, 1)
                act.activation(rc[:], rx[:], ACT.Sin).then_inc(i_act, 1)

        p_tok = y_f[:, 0:2, :].rearrange("p a s -> p (a s)").rearrange("p (t c) -> p t c", t=NQ)
        tile_of = {x_[:2]: t for t, x_ in enumerate(tiles)}
        names = ("par_ld par2_ld pe_par pe_norm act_norm dve_norm h_hi_s h_lo_s act_hi dve_lo pe_dense act_evac "
                 "dve_evac dve_chain pool_rot dve_rm dve_rs act_rot qk_s pe_s dve_max act_exp dve_comb pe_t "
                 "pt_act_s pt_dve_s pe_v dve_norm_o yq_s yqc_s pe_misc dve_misc dve_ysplit act_ys dve_hid act_hid dve_hx "
                 "lf_s act_lf lam_s act_lam ck_s cs_s act_cx cprob_s ms_s pool_pow act_msq act_merge dve_merge "
                 "zero_s act_x1 x1_s dve_acc dve_x act_sq pool_sum p_ld pe_p dve_p act_p flat_s act_flat").split()
        sw_ld = sem("sw_ld")
        LSW = 64 * len(rots)
        sems_before = len(sems)
        M = {n: sem(n) for n in names}
        raw_ld = [sem(f"raw_ld{j}") for j in range(RAW)]
        layer_sems = sems[sems_before:]

        def pt_wait(eng, k):
            if k in pt_act.order:
                eng.wait_ge(M["pt_act_s"], pt_act.after(k))
            else:
                eng.wait_ge(M["pt_dve_s"], pt_dve.after(k))

        def copy_pt(eng, k):
            n = (prob_rows[k][1] + 1) * P
            eng.wait_ge(M["pe_t"], k + 1)
            if k >= 2:
                eng.wait_ge(M["pe_v"], k - 1)
            if k in pt_act.order:
                eng.activation(pT[:, k % 2, 0:n], Tr[k % 2][:, 0:n], ACT.Copy).then_inc(M["pt_act_s"], 1)
            else:
                eng.tensor_copy(pT[:, k % 2, 0:n], Tr[k % 2][:, 0:n]).then_inc(M["pt_dve_s"], 1)

        def kind_of(t):
            if t < T0:
                return tiles[t][0]
            if t < T1:
                return ("mgc", "brc")[(t - T0) % 2]
            if t < T2:
                return "out"
            return ("gate", "ple")[(t - T2) % 2]

        def landed_at(t):
            if t < T0:
                return landed[t]
            return slot_sum[t % RAW] + 16 * ((t - T0) // RAW + 1)

        def rot_dst(kind, n):
            if kind == "ksb":
                return ks_hi, ks_lo, None
            if kind == "kwb":
                return kw_hi, kw_lo, None
            u = (4 if kind == "qb" else 8) + n
            return (k_hi[u % 2], k_lo[u % 2], u) if kind == "kc" else (q_hi[u % 2], q_lo[u % 2], u)

        with nc.Fori(0, DEPTH) as L:
            with nc.Block() as block:

                @block.sync
                def _(sp):
                    rows_ = [(norm_g[bass.ds(L, 1), :].rearrange("a (m p) -> (a m) p", p=P), 0, 8),
                             (cmp_b1_k[bass.ds(L, 1), :].rearrange("a (m p) -> (a m) p", p=P), 8, 2),
                             (cmp_b1_v[bass.ds(L, 1), :].rearrange("a (m p) -> (a m) p", p=P), 10, 2),
                             (cmp_pe_k[bass.ds(L, 1)].rearrange("a (m two) d -> (a m) (two d)", two=2), 12, 16),
                             (cmp_pe_v[bass.ds(L, 1)].rearrange("a (m two) d -> (a m) (two d)", two=2), 28, 16),
                             (diff_subln_g[bass.ds(L, 1), :], 44, 1)]
                    for src, r, n in rows_:
                        sp.dma_start(prow[r:r + n, :], src).then_inc(M["par_ld"], 16)

                    def load(L, kind, n, t):
                        for ps, cs, src in sources(L, kind, n):
                            dst = raw[ps, t % RAW, 0:kt(kind) * P].rearrange("p (k n) -> p k n", n=P)[:, :, cs]
                            sp.dma_start(dst, src).then_inc(raw_ld[t % RAW], 16)

                    def static_load(t):
                        if t >= RAW:
                            sp.wait_ge(M["dve_lo"], t - RAW + 1)
                        if t < T0:
                            load(L, tiles[t][0], tiles[t][1], t)
                        else:
                            load(L, ("mgc", "brc")[(t - T0) % 2], (t - T0) // 2, t)
                    for t in range(2):
                        static_load(t)
                    small = [(w2k[:, :, 0:HD], cmp_w2_k[bass.ds(L, 1)].rearrange("a (k p) n -> p (a k) n", p=P)),
                             (w2k[:, :, HD:P], cmp_w2_k[bass.ds(L, 1)].rearrange("a (k p) n -> p (a k) n", p=P)),
                             (w2v, cmp_w2_v[bass.ds(L, 1)].rearrange("a (k p) n -> p (a k) n", p=P)),
                             (bfor[:], b_forget[bass.ds(L, 1), :].rearrange("a h -> h a")),
                             (lamr, diff_lam[bass.ds(L, 1)].rearrange("a f d -> a (f d)").to_broadcast([P, 4 * HD])),
                             (lconst[:], layer_consts[bass.ds(L, 1)].rearrange("a p c -> (a p) c"))]
                    for dst, src in small:
                        sp.dma_start(dst, src).then_inc(M["par2_ld"], 16)
                    for t in range(2, 6):
                        static_load(t)
                    for it in items:
                        if it[0] == "end" and it[1] + 6 < T0 + 4:
                            static_load(it[1] + 6)
                    sp.wait_ge(M["dve_ysplit"], 12)
                    sp.dma_start(p_tok, p[bass.ds(L, 1)].rearrange("a b (t p) c -> p (a b t) c", p=P)).then_inc(M["p_ld"], 16)
                    with sp.Fori(0, NM // 2 - 1) as i:
                        for j in range(4):
                            t = T0 + 4 + j
                            sp.wait_ge(M["dve_lo"], i * 4 + (t - RAW + 1))
                            load(L, ("mgc", "brc")[j % 2], i * 2 + (2 + j // 2), t)
                    with sp.Fori(0, NM // 4) as i:
                        for j in range(4):
                            t = T1 + j
                            sp.wait_ge(M["dve_lo"], i * 4 + (t - RAW + 1))
                            load(L, "out", i * 4 + j, t)
                    with sp.Fori(0, NM // 2) as i:
                        for j in range(4):
                            t = T2 + j
                            sp.wait_ge(M["dve_lo"], i * 4 + (t - RAW + 1))
                            load(L, ("gate", "ple")[j % 2], i * 2 + j // 2, t)

                @block.gpsimd
                def _(pool):
                    pool.memset(flat, 0.0).then_inc(M["zero_s"], 1)
                    for m in range(NM):
                        pool.wait_ge(M["h_hi_s"], m + 1)
                        pool.tensor_tensor(h_lo[:, m, :], th[:, m % 2, :], f(h_hi[:, m, :]),
                                           ALU.subtract).then_inc(M["h_lo_s"], 1)
                    for it in items:
                        if it[0] == "end" and tiles[it[1]][0] in ROTATED:
                            t = it[1]
                            src = qf if tiles[t][0] == "qb" else rx
                            n = rots.after(t)
                            pool.wait_ge(M["act_evac"], act_evac.after(t))
                            if n > 1:
                                pool.wait_ge(M["pool_rot"], n - 1)
                            for a, b in ((0, 32), (32, 0), (64, 96), (96, 64)):
                                pool.dma_start(rs[a:a + 32, :], src[b:b + 32, :]).then_inc(sw_ld, 16)
                            pool.wait_ge(sw_ld, L * LSW + 64 * n)
                            if n > 1:
                                pool.wait_ge(M["dve_rs"], n - 1)
                            pool.tensor_tensor(rb[:], rs[:], sinT[:], ALU.mult).then_inc(M["pool_rot"], 1)
                        if it[0] == "MS":
                            pool.wait_ge(M["ms_s"], it[1] - 7)
                            pool.tensor_tensor(msq[:, 2, :], msq[:, 1, :], halfs[:], ALU.pow).then_inc(M["pool_pow"], 1)
                    pool.wait_ge(M["dve_merge"], 1)
                    pool.memset(ssum[:], 0.0).then_inc(M["pool_sum"], 1)
                    with pool.Fori(0, NM // 2) as i:
                        for j in range(2):
                            pool.wait_ge(M["act_sq"], i * 2 + (j + 1))
                            pool.wait_ge(M["pool_sum"], i * 2 + (j + 1))
                            pool.tensor_tensor(ssum[:], ssum[:], probs[:, j, :], ALU.add).then_inc(M["pool_sum"], 1)

                @block.tensor
                def _(pe):
                    pe.matmul(Mb[:], ones[:], ssum[:], start=True, stop=True).then_inc(M["pe_norm"], 1)
                    pe.wait_ge(M["par_ld"], 96)
                    pe.transpose(Ob[:, 0:45], prow[0:45, :], ident[0:45, 0:45]).then_inc(M["pe_par"], 1)

                    moving = {"w1k": (flat_hi, flat_lo), "w1v": (flat_hi, flat_lo), "bra": (y_hi, y_lo),
                              "brb": (y_hi, y_lo), "brc": (y_hi, y_lo), "ple": (y_hi, y_lo),
                              "out": (h_hi, h_lo), "gate": (x1_hi, x1_lo)}

                    def dense(kind, t, k, width=S, k0=0):
                        hi, lo = moving.get(kind, (h_hi, h_lo))
                        cs = slice(k * P, (k + 1) * P)
                        o = Dn[t % 2][:, 0:width]
                        sl = t % SPL
                        last = k == kt(kind) - 1
                        pe.matmul(o, w_hi[:, sl, cs], hi[:, k0 + k, :], start=(k == 0), stop=False)
                        pe.matmul(o, w_lo[:, sl, cs], hi[:, k0 + k, :], start=False, stop=False)
                        ins = pe.matmul(o, w_hi[:, sl, cs], lo[:, k0 + k, :], start=False, stop=last)
                        if last:
                            ins.then_inc(M["pe_dense"], 1)

                    def bank_free(t):
                        if t < 2:
                            return
                        kind = tiles[t - 2][0]
                        if kind in DVE_EVAC:
                            pe.wait_ge(M["dve_evac"], dve_evac.after(t - 2))
                        else:
                            pe.wait_ge(M["act_evac"], act_evac.after(t - 2))

                    def misc_free(it):
                        n = misc.after(it)
                        if n > 1:
                            pe.wait_ge(M["dve_misc"], n - 1)

                    for it in items:
                        what = it[0]
                        if what == "mm":
                            t, k = it[1:]
                            kind, n, _ = tiles[t]
                            if k == 0:
                                bank_free(t)
                                pe.wait_ge(M["dve_lo"], t + 1)
                                if kind in ("w1k", "w1v") and n == 0:
                                    pe.wait_ge(M["flat_s"], 1 if kind == "w1k" else 2)
                                if kind in ("bra", "brb") and n == 0:
                                    pe.wait_ge(M["dve_ysplit"], 4 if kind == "bra" else 8)
                            if t == 0:
                                pe.wait_ge(M["h_lo_s"], k + 1)
                            if kind in ("w1k", "w1v"):
                                dense(kind, t, k, 2 * C32, 8 * (n % 2))
                            else:
                                dense(kind, t, k)
                        elif what == "gates":
                            misc_free(it)
                            pe.wait_ge(M["act_evac"], act_evac.after(it[1]))
                            for i in range(NQ):
                                ins = pe.transpose(Mb[:, i * P:(i + 1) * P], th[:, 0, i * P:(i + 1) * P], ident[:])
                            ins.then_inc(M["pe_misc"], 1)
                        elif what == "vt":
                            misc_free(it)
                            pe.wait_ge(M["act_evac"], act_evac.after(it[1]))
                            for i in range(NQ):
                                ins = pe.transpose(Mb[:, i * P:(i + 1) * P], vT[:, i * P:(i + 1) * P], ident[:])
                            ins.then_inc(M["pe_misc"], 1)
                        elif what == "kcmp":
                            misc_free(it)
                            pe.wait_ge(M["dve_hid"], hids.after(("w1k", 3)))
                            pe.wait_ge(M["par2_ld"], 96)
                            for ht in range(2):
                                ins = pe.matmul(Mb[:, 0:64], w2k[:, ht, :], hid[:, ht, :, 0, :], start=(ht == 0), stop=(ht == 1))
                            ins.then_inc(M["pe_misc"], 1)
                        elif what == "vcmp":
                            misc_free(it)
                            pe.wait_ge(M["dve_hid"], hids.after(("w1v", 3)))
                            for g in range(2):
                                for ht in range(2):
                                    ins = pe.matmul(Mb[:, HD * g:HD * g + HD], hid[:, ht, g].rearrange("p b c -> p (b c)"),
                                                    w2v[:, ht, :], start=(ht == 0), stop=(ht == 1))
                            ins.then_inc(M["pe_misc"], 1)
                        elif what == "cs":
                            u = it[1]
                            misc_free(it)
                            if u == 4:
                                pe.wait_ge(M["dve_misc"], misc.after(("kcmp", tile_of[("w1k", 3)])))
                                pe.wait_ge(M["dve_misc"], misc.after(("vcmp", tile_of[("w1v", 3)])))
                            pe.wait_ge(M["act_evac"], act_evac.after(tile_of[("qb", u - 4)]))
                            for i in range(NQ):
                                ins = pe.matmul(Mb[:, 2 * C32 * i:2 * C32 * (i + 1)], qf[:, i * P:(i + 1) * P], kcmpT[:],
                                                start=True, stop=True)
                            ins.then_inc(M["pe_misc"], 1)
                        elif what == "ct":
                            misc_free(it)
                            pe.wait_ge(M["cprob_s"], it[1] - 3)
                            for g in range(2):
                                ins = pe.transpose(Mb[:, g * P:(g + 1) * P],
                                                   pc[:, 2 * g:2 * g + 2].rearrange("p i h c -> p (i h c)"), ident[:])
                            ins.then_inc(M["pe_misc"], 1)
                        elif what == "S":
                            r = it[1]
                            u, i, m, h = rows[r]
                            b = u % 2
                            if i == 0 and h == 0:
                                if m == "a":
                                    pe.wait_ge(M["dve_evac"], dve_evac.after(tile_of[("ka", u)]))
                                    if u == 0:
                                        pe.wait_ge(M["ck_s"], 2)
                                elif m == "c":
                                    pe.wait_ge(M["qk_s"], qk_ready.after(("kc", u - 8)))
                                elif m == "sel":
                                    pe.wait_ge(M["qk_s"], qk_ready.after(("qb", u - 4)))
                            if r >= 2:
                                pe.wait_ge(M["act_exp"], r - 1)
                            ps = slice(HD * h, HD * h + HD)
                            ka, kb = {"a": (k_hi[b], k_lo[b]), "c": (k_hi[b], k_lo[b]),
                                      "sel": (ks_hi, ks_lo), "win": (kw_hi, kw_lo)}[m]
                            n = (i + 1) * P
                            o = Sc[r % 2][:, 0:n]
                            qs = slice(i * P, n)
                            pe.matmul(o, q_hi[b][ps, qs], ka[ps, 0:n], start=True, stop=False)
                            pe.matmul(o, q_lo[b][ps, qs], ka[ps, 0:n], start=False, stop=False)
                            pe.matmul(o, q_hi[b][ps, qs], kb[ps, 0:n], start=False, stop=False)
                            if m == "a":
                                hh = 2 * u + h
                                pe.matmul(o, selr[:, hh:hh + 1].to_broadcast([P, P]), ck[:, 0:n], start=False, stop=False)
                            pe.matmul(Sc[r % 2][:, qs], identb[:], maskb[:], start=False, stop=True).then_inc(M["pe_s"], 1)
                        elif what == "T":
                            k = it[1]
                            u, i, m, h, r, _ = prob_rows[k]
                            if m == "c":
                                pe.wait_ge(M["dve_comb"], NQ * (u - 8) + i + 1)
                            else:
                                pe.wait_ge(M["act_exp"], r + 1)
                            if k >= 2:
                                pt_wait(pe, k - 2)
                            src = probs[:, (r - 1 if m == "c" else r) % NP_, :]
                            for j in range(i + 1):
                                ins = pe.transpose(Tr[k % 2][:, j * P:(j + 1) * P], src[:, j * P:(j + 1) * P], ident[:])
                            ins.then_inc(M["pe_t"], 1)
                        elif what == "V":
                            k = it[1]
                            u, i, m, h, r, last = prob_rows[k]
                            pt_wait(pe, k)
                            o = NQ * u + i
                            if k == first_prob[(u, i)]:
                                if o:
                                    pe.wait_ge(M["dve_norm_o"], o)
                                if i == 0 and u in (0, 4, 8):
                                    lastv = {0: ("va", 3), 4: ("vwb", 0), 8: ("vc", 3)}[u]
                                    pe.wait_ge(M["dve_misc"], misc.after(("vt", tile_of[lastv])))
                            if m == "c":
                                oc, vs = slice(0, P), lambda j: v_ac[:, j, (u - 8) * P:(u - 7) * P]
                            elif m == "a":
                                oc, vs = slice(HD * h, HD * h + HD), lambda j: v_ac[:, j, (2 * u + h) * HD:(2 * u + h + 1) * HD]
                            else:
                                bi = 1 if m == "sel" else 2
                                c0 = (bi - 1) * P + HD * h
                                oc, vs = slice(bi * P + HD * h, bi * P + HD * h + HD), lambda j: v_b[:, j, c0:c0 + HD]
                            for j in range(i + 1):
                                ins = pe.matmul(Ob[:, oc], pT[:, k % 2, j * P:(j + 1) * P], vs(j), start=(j == 0), stop=(j == i))
                            if last and branch(u) == "B":
                                if i == 0:
                                    pe.wait_ge(M["dve_misc"], misc.after(("ct", u)))
                                hs = slice(64 * (i % 2), 64 * (i % 2) + 64)
                                ins = pe.matmul(Ob[:, 0:P], pcT[hs, i // 2, :], vbd[hs, :], start=True, stop=True)
                            ins.then_inc(M["pe_v"], 1)
                        elif what == "Y":
                            u = it[1]
                            misc_free(it)
                            if branch(u) == "C":
                                pe.wait_ge(M["yqc_s"], u - 7)
                            elif branch(u) == "B":
                                pe.wait_ge(M["yq_s"], NQ * (u - 3))
                            else:
                                pe.wait_ge(M["dve_norm_o"], NQ * (u + 1))
                            for i in range(NQ):
                                ins = pe.transpose(Mb[:, i * P:(i + 1) * P], y_q[:, i, :], ident[:])
                            ins.then_inc(M["pe_misc"], 1)

                    pe.wait_ge(M["dve_ysplit"], 12)
                    with pe.Fori(0, NM // 2) as i:
                        for j in range(4):
                            t = T0 + j
                            kind = ("mgc", "brc")[j % 2]
                            if kind == "mgc":
                                pe.wait_ge(M["act_evac"], i * 2 + (AE0 + j // 2))
                            else:
                                pe.wait_ge(M["dve_evac"], i * 2 + (DE0 + j // 2))
                            pe.wait_ge(M["dve_lo"], i * 4 + (t + 1))
                            for k in range(kt(kind)):
                                dense(kind, t, k)
                    pe.wait_ge(M["p_ld"], 16)
                    for c, b in ((0, Mb), (1, Ob)):
                        for t in range(NQ):
                            ins = pe.transpose(b[:, t * P:(t + 1) * P], p_tok[:, t, c * P:(c + 1) * P], ident[:])
                        ins.then_inc(M["pe_p"], 1)
                    pe.wait_ge(M["act_evac"], AE1)
                    with pe.Fori(0, NM // 4) as i:
                        for j in range(4):
                            t = T1 + j
                            pe.wait_ge(M["dve_evac"], i * 4 + (DE1 + j - 1))
                            pe.wait_ge(M["dve_lo"], i * 4 + (t + 1))
                            for k in range(NM):
                                if j == 0:
                                    pe.wait_ge(M["dve_merge"], k + 1)
                                dense("out", t, k)
                    pe.wait_ge(M["dve_p"], 2)
                    with pe.Fori(0, NM // 2) as i:
                        for j in range(4):
                            t = T2 + j
                            kind = ("gate", "ple")[j % 2]
                            if kind == "gate":
                                pe.wait_ge(M["act_evac"], i * 2 + (AE1 + j // 2))
                                if j == 0:
                                    pe.wait_ge(M["dve_evac"], i * 2 + (DE2 - 1))
                            else:
                                pe.wait_ge(M["dve_evac"], i * 2 + (DE2 + j // 2))
                            pe.wait_ge(M["dve_lo"], i * 4 + (t + 1))
                            for k in range(kt(kind)):
                                if j == 0:
                                    pe.wait_ge(M["x1_s"], k + 1)
                                dense(kind, t, k)

                @block.scalar
                def _(act):
                    A = act.activation
                    act.wait_ge(M["dve_norm"], 1)
                    A(rx[:], rb[:], ACT.Ln).then_inc(M["act_norm"], 1)
                    act.wait_ge(M["act_norm"], 1)
                    A(rs[:], rx[:], ACT.Exp, scale=-0.5).then_inc(M["act_norm"], 1)
                    for m in range(NM):
                        act.wait_ge(M["dve_norm"], 6 + m + 1)
                        A(h_hi[:, m, :], th[:, m % 2, :], ACT.Copy).then_inc(M["h_hi_s"], 1)

                    def hi(t, i=None, k=8):
                        sl, n = t % SPL, (kt(kind_of(t)) if i is None else k) * P
                        if i is None:
                            act.wait_ge(raw_ld[t % RAW], landed_at(t))
                            if t >= SPL:
                                act.wait_ge(M["pe_dense"], t - SPL + 1)
                        else:
                            act.wait_ge(raw_ld[t % RAW], i * 16 + landed_at(t))
                            act.wait_ge(M["pe_dense"], i * 4 + (t - SPL + 1))
                        A(w_hi[:, sl, 0:n], raw[:, t % RAW, 0:n], ACT.Copy).then_inc(M["act_hi"], 1)

                    hi(0)
                    hi(1)
                    th_free = []
                    last_vt = None
                    for it in items:
                        what = it[0]
                        if what == "end":
                            t = it[1]
                            kind, n, s = tiles[t]
                            D = Dn[t % 2]
                            hi(t + 2)
                            if kind in ACT_EVAC:
                                act.wait_ge(M["pe_dense"], t + 1)
                            if kind in ("fg", "za", "zb", "zc", "mga", "mgb"):
                                c = len(th_free)
                                if c == 0:
                                    act.wait_ge(M["h_lo_s"], NM)
                                if c >= 2:
                                    act.wait_ge(*th_free[c - 2])
                                if kind == "fg":
                                    th_free.append((M["pe_misc"], 1))
                                elif kind[0] == "z":
                                    th_free.append((M["dve_evac"], dve_evac.after(t)))
                                else:
                                    th_free.append((M["dve_evac"], dve_evac.after(tile_of[("br" + kind[2], n)])))
                                A(th[:, c % 2, :], D[:], ACT.Tanh, scale=0.5).then_inc(M["act_evac"], 1)
                            if kind == "fg":
                                act.wait_ge(M["lf_s"], 1)
                                A(lf[:, 2, :], lf[:, 1, :], ACT.Exp, scale=-1.0).then_inc(M["act_lf"], 1)
                                act.wait_ge(M["act_lf"], 1)
                                A(lf[:, 3, :], lf[:, 2, :], ACT.Ln, bias=1.0).then_inc(M["act_lf"], 1)
                            if kind in ("qa", "ka"):
                                if n >= 2:
                                    act.wait_ge(M["pe_s"], rows_before[n - 1])
                                dst = (q_hi if kind == "qa" else k_hi)[n % 2]
                                A(dst, D[:], ACT.Copy, scale=QSCALE if kind == "qa" else 1.0).then_inc(M["act_evac"], 1)
                            if kind in ROTATED:
                                r = rots.after(t)
                                if r > 1:
                                    act.wait_ge(sw_ld, L * LSW + 64 * (r - 1))
                                    act.wait_ge(M["dve_rm"], r - 1)
                                if kind == "qb" and n:
                                    act.wait_ge(M["pe_misc"], misc.after(("cs", 3 + n)))
                                dst = qf if kind == "qb" else rx
                                A(dst[:], D[:], ACT.Copy, scale=QSCALE if kind[0] == "q" else 1.0).then_inc(M["act_evac"], 1)
                            if kind in VALUES:
                                if last_vt is not None:
                                    act.wait_ge(M["pe_misc"], misc.after(("vt", last_vt)))
                                last_vt = t
                                A(vT, D[:], ACT.Copy).then_inc(M["act_evac"], 1)
                            if kind in ("kcb", "vcb"):
                                c = 0 if kind == "kcb" else 1
                                act.wait_ge(M["dve_evac"], dve_evac.after(t))
                                if c:
                                    act.wait_ge(M["pe_dense"], tile_of[("w1k", 3)] + 1)
                                A(flat_hi, flat, ACT.Copy).then_inc(M["act_flat"], 1)
                            if kind in ("w1k", "w1v") and n % 2:
                                act.wait_ge(M["dve_evac"], dve_evac.after(t))
                                A(hth, hacc[:, 1, :], ACT.Tanh, scale=0.5).then_inc(M["act_hid"], 1)
                        elif what == "gates":
                            act.wait_ge(M["lam_s"], 1)
                            A(lams[:, 2:4], lams[:, 0:2], ACT.Exp).then_inc(M["act_lam"], 1)
                        elif what == "rot":
                            t = it[1]
                            kind, n, s = tiles[t]
                            hi_, lo_, u = rot_dst(kind, n)
                            act.wait_ge(M["dve_rs"], rots.after(t))
                            if u is not None and u >= 2:
                                act.wait_ge(M["pe_s"], rows_before[u - 1])
                            A(hi_, rc[:], ACT.Copy).then_inc(M["act_rot"], 1)
                        elif what == "S":
                            r = it[1]
                            u, i, m, h = rows[r]
                            n = (i + 1) * P
                            c = {"a": 0, "c": 0, "sel": 2, "win": 4}[m] + h
                            act.wait_ge(M["dve_max"], r + 1)
                            if r >= NP_:
                                act.wait_ge(M["pe_t"], prob_of_row[r - NP_] + 1)
                            A(probs[:, r % NP_, 0:n], Sc[r % 2][:, 0:n], ACT.Exp, bias=nmax[:, r % 8:r % 8 + 1],
                              accum_out=sums[:, u % 2, i, c:c + 1]).then_inc(M["act_exp"], 1)
                        elif what == "T" and it[1] in pt_act.order:
                            copy_pt(act, it[1])
                        elif what == "cs":
                            act.wait_ge(M["cs_s"], it[1] - 3)
                            if it[1] > 4:
                                act.wait_ge(M["pe_misc"], misc.after(("ct", it[1] - 1)))
                            A(pc[:], cs_[:], ACT.Exp).then_inc(M["act_cx"], 1)
                        elif what == "N" and branch(it[1] // NQ) == "C":
                            u, i = divmod(it[1], NQ)
                            act.wait_ge(M["dve_norm_o"], it[1] + 1)
                            A(sqj, y_q[:, i, :], ACT.Square, accum_out=msq[:, 0, i:i + 1]).then_inc(M["act_msq"], 1)
                            act.wait_ge(M["act_msq"], NQ * (u - 8) + i + 1)
                        elif what == "YS":
                            u = it[1]
                            act.wait_ge(M["dve_misc"], misc.after(("Y", u)))
                            if u >= 4:
                                act.wait_ge(M["pe_dense"], tile_of[(("bra", "brb")[u // 4 - 1], NM - 1)] + 1)
                            A(y_hi[:, u % 4, :], y_f[:, y_slot(u), :], ACT.Copy).then_inc(M["act_ys"], 1)

                    with act.Fori(0, NM // 2) as i:
                        for j in range(4):
                            t = T0 + j
                            hi(t + 2, i)
                            if j % 2 == 0:
                                act.wait_ge(M["pe_dense"], i * 4 + (t + 1))
                                act.wait_ge(M["dve_evac"], i * 2 + (DE0 + j // 2 - 1))
                                A(th[:, j // 2, :], Dn[t % 2][:], ACT.Tanh, scale=0.5).then_inc(M["act_evac"], 1)
                    for m in range(NM):
                        if m == 0:
                            act.wait_ge(M["pe_dense"], T1)
                        act.wait_ge(M["dve_acc"], DA0 + m + 1)
                        A(h_hi[:, m, :], acc[:, m, :], ACT.Copy, scale=0.5).then_inc(M["act_merge"], 1)
                    for c, b in ((0, Mb), (1, Ob)):
                        act.wait_ge(M["pe_p"], c + 1)
                        A(y_hi[:, c, :], b[:], ACT.Copy).then_inc(M["act_p"], 1)
                    with act.Fori(0, NM // 4) as i:
                        for j in range(4):
                            t = T1 + j
                            hi(t + 2, i)
                            act.wait_ge(M["dve_evac"], i * 4 + (DE1 + j + 1))
                            A(x1_hi[:, bass.ds(i * 4 + j, 1), :].rearrange("p a s -> p (a s)"),
                              xT[:, bass.ds(i * 4 + j, 1), :].rearrange("p a s -> p (a s)"), ACT.Copy).then_inc(M["act_x1"], 1)

                    def gate_tiles(i, m0, ahead):
                        for j in range(4):
                            t = T2 + 2 * m0 + j
                            if ahead or j < 2:
                                hi(t + 2, i, kt(("gate", "ple")[j % 2]))
                            if j % 2 == 0:
                                act.wait_ge(M["pe_dense"], i * 4 + (t + 1))
                                act.wait_ge(M["dve_evac"], i * 2 + (DE2 + m0 + j // 2 - 1))
                                A(th[:, j // 2, :], Dn[t % 2][:], ACT.Tanh, scale=0.5).then_inc(M["act_evac"], 1)
                            else:
                                act.wait_ge(M["dve_x"], i * 2 + (m0 + j // 2 + 1))
                                act.wait_ge(M["pool_sum"], i * 2 + (m0 + j // 2 + 1))
                                A(probs[:, j // 2, :], xT[:, bass.ds(i * 2 + (m0 + j // 2), 1), :].rearrange("p a s -> p (a s)"),
                                  ACT.Square).then_inc(M["act_sq"], 1)
                    with act.Fori(0, NM // 2 - 1) as i:
                        gate_tiles(i, 0, True)
                    gate_tiles(0, NM - 2, False)

                @block.vector
                def _(dve):
                    chained = 0

                    def link(ins):
                        nonlocal chained
                        chained += 1
                        ins.then_inc(M["dve_chain"], 1)
                        dve.wait_ge(M["dve_chain"], chained)

                    TT, STT, TS, RED = dve.tensor_tensor, dve.scalar_tensor_tensor, dve.tensor_scalar, dve.tensor_reduce

                    dve.wait_ge(M["pe_norm"], 1)
                    TS(rb[:], Mb[:], 1.0 / D, EPS, ALU.mult, ALU.add).then_inc(M["dve_norm"], 1)
                    dve.wait_ge(M["pe_par"], 1)
                    dve.tensor_copy(par[:, 0:45], Ob[:, 0:45]).then_inc(M["dve_norm"], 1)
                    dve.wait_ge(M["act_norm"], 2)
                    TT(rc[:], rs[:], rs[:], ALU.mult).then_inc(M["dve_norm"], 1)
                    dve.wait_ge(M["dve_norm"], 3)
                    TT(rc[:], rc[:], rb[:], ALU.mult).then_inc(M["dve_norm"], 1)
                    dve.wait_ge(M["dve_norm"], 4)
                    TS(rc[:], rc[:], -0.5, 1.5, ALU.mult, ALU.add).then_inc(M["dve_norm"], 1)
                    dve.wait_ge(M["dve_norm"], 5)
                    TT(rs[:], rs[:], rc[:], ALU.mult).then_inc(M["dve_norm"], 1)
                    dve.wait_ge(M["dve_norm"], 6)
                    for m in range(NM):
                        if m >= 2:
                            dve.wait_ge(M["h_lo_s"], m - 1)
                        STT(th[:, m % 2, :], xT[:, m, :], par[:, m:m + 1], rs[:], ALU.mult, ALU.mult).then_inc(M["dve_norm"], 1)

                    def lo(t, i=None, k=8):
                        sl, n = t % SPL, (kt(kind_of(t)) if i is None else k) * P
                        if i is None:
                            dve.wait_ge(M["act_hi"], t + 1)
                        else:
                            dve.wait_ge(M["act_hi"], i * 4 + (t + 1))
                        TT(w_lo[:, sl, 0:n], raw[:, t % RAW, 0:n], f(w_hi[:, sl, 0:n]), ALU.subtract).then_inc(M["dve_lo"], 1)

                    lo(0)
                    lo(1)
                    for it in items:
                        what = it[0]
                        if what == "end":
                            t = it[1]
                            kind, n, s = tiles[t]
                            Db = Dn[t % 2]
                            lo(t + 2)
                            if kind in DVE_EVAC:
                                dve.wait_ge(M["pe_dense"], t + 1)
                                if kind in ACT_EVAC:
                                    dve.wait_ge(M["act_evac"], act_evac.after(t))
                            done = M["dve_evac"]
                            if kind == "fg":
                                dve.wait_ge(M["par2_ld"], 96)
                                TS(lf[:, 0, :], Db[0:8, :], bfor[:, 0:1], None, ALU.add).then_inc(done, 1)
                                dve.wait_ge(done, dve_evac.after(t))
                                link(TS(lf[:, 1, :], lf[:, 0, :], -1.0, None, ALU.mult))
                                TT(lf[:, 1, :], lf[:, 1, :], lf[:, 0, :], ALU.max).then_inc(M["lf_s"], 1)
                                dve.wait_ge(M["act_lf"], 2)
                                link(TS(lf[:, 0, :], lf[:, 0, :], 0.0, None, ALU.min))
                                link(TS(lf[:, 2, :], lf[:, 0, :], 0.0, None, ALU.mult))
                                link(TT(lf[:, 0, :], lf[:, 0, :], lf[:, 3, :], ALU.subtract))
                                link(dve.tensor_tensor_scan(lf[:, 1, :], lf[:, 2, :], lf[:, 0, :], 0.0, ALU.add, ALU.add))
                                TS(ck[0:8, :], lf[:, 1, :], -1.0, None, ALU.mult).then_inc(M["ck_s"], 1)
                                dve.wait_ge(M["ck_s"], 1)
                                STT(ck[32:40, :], lf[:, 1, :], -1.0, f(ck[0:8, :]), ALU.mult, ALU.subtract).then_inc(M["ck_s"], 1)
                            elif kind in ("qa", "ka"):
                                src, dst = (q_hi, q_lo) if kind == "qa" else (k_hi, k_lo)
                                STT(dst[n % 2], Db[:], QSCALE if kind == "qa" else 1.0, f(src[n % 2]),
                                    ALU.mult, ALU.subtract).then_inc(done, 1)
                            elif kind in ("za", "zb", "zc"):
                                slot = th_slot[t]
                                STT(zs[:], th[:, slot, :], 1.0, Db[:], ALU.add, ALU.mult).then_inc(done, 1)
                            elif kind in ROTATED:
                                r = rots.after(t)
                                dve.wait_ge(M["act_evac"], act_evac.after(t))
                                if r > 1:
                                    dve.wait_ge(M["qk_s"], r - 1)
                                TT(rc[:], (qf if kind == "qb" else rx)[:], cosT[:], ALU.mult).then_inc(M["dve_rm"], 1)
                            elif kind in ("kcb", "vcb"):
                                if kind == "vcb":
                                    dve.wait_ge(M["flat_s"], 1)
                                else:
                                    dve.wait_ge(M["zero_s"], 1)
                                p0 = 12 if kind == "kcb" else 28
                                for g in range(2):
                                    tok = Db[HD * g:HD * g + HD, :].rearrange("p (c s) -> p s c", s=CS)
                                    for par_ in range(2):
                                        ps = slice(HD * par_, HD * par_ + HD)
                                        for mh in range(2):
                                            ins = TT(flat[ps, 8 * mh:8 * mh + 8, C32 * g:C32 * g + NC],
                                                     tok[:, par_:CS:2, mh:mh + NC],
                                                     par[ps, p0 + 8 * mh:p0 + 8 * mh + 8].unsqueeze(2).to_broadcast([HD, 8, NC]),
                                                     ALU.add)
                                ins.then_inc(done, 1)
                                dve.wait_ge(M["act_flat"], 1 if kind == "kcb" else 2)
                                TT(flat_lo, flat, f(flat_hi), ALU.subtract).then_inc(M["flat_s"], 1)
                            elif kind in ("w1k", "w1v"):
                                ht = n // 2
                                if n % 2 == 0:
                                    dve.tensor_copy(hacc[:, 0, :], Db[:, 0:64]).then_inc(done, 1)
                                else:
                                    b1 = (8 if kind == "w1k" else 10) + ht
                                    dve.wait_ge(done, dve_evac.after(tile_of[(kind, n - 1)]))
                                    STT(hacc[:, 1, :], Db[:, 0:64], par[:, b1:b1 + 1], hacc[:, 0, :], ALU.add, ALU.add).then_inc(done, 1)
                                    dve.wait_ge(M["act_hid"], hids.after((kind, n)))
                                    if kind == "w1v":
                                        dve.wait_ge(M["pe_misc"], misc.after(("kcmp", tile_of[("w1k", 3)])))
                                    for g in range(2):
                                        cs = slice(C32 * g, C32 * g + C32)
                                        ins = STT(hid[:, ht, g], hth[:, cs].unsqueeze(1).to_broadcast([P, 4, C32]), 1.0,
                                                  hacc[:, 1, cs].unsqueeze(1).to_broadcast([P, 4, C32]), ALU.add, ALU.mult)
                                    ins.then_inc(M["dve_hid"], 1)
                            elif kind in ("bra", "brb"):
                                first = kind == "bra"
                                dst = acc[:, n, :] if first else rt[:]
                                dve.wait_ge(M["act_evac"], act_evac.after(tile_of[("mg" + kind[2], n)]))
                                STT(dst, th[:, th_slot[tile_of[("mg" + kind[2], n)]], :], 1.0, Db[:],
                                    ALU.add, ALU.mult).then_inc(done, 1)
                                if not first:
                                    dve.wait_ge(done, dve_evac.after(t))
                                    TT(acc[:, n, :], acc[:, n, :], rt[:], ALU.add).then_inc(M["dve_acc"], 1)
                        elif what == "gates":
                            dve.wait_ge(M["pe_misc"], misc.after(it))
                            TS(gates[:], Mb[:].rearrange("p (i c) -> p i c", i=NQ)[:, :, 32:56], 0.5, 0.5,
                               ALU.mult, ALU.add).then_inc(M["dve_misc"], 1)
                            lv = lamr.rearrange("p (a two d) -> p a two d", a=2, two=2)
                            link(TT(tmp[:, 2 * P:3 * P].rearrange("p (a d) -> p a d", a=2), lv[:, :, 0, :], lv[:, :, 1, :], ALU.mult))
                            RED(lams[:, 0:2], tmp[:, 2 * P:3 * P].rearrange("p (a d) -> p a d", a=2), AX.X, ALU.add).then_inc(M["lam_s"], 1)
                            link(TT(gsc[:], par[:, 44:45], lconst[:, 1:2], ALU.mult))
                            dve.wait_ge(M["act_lam"], 1)
                            link(TT(lams[:, 4:5], lams[:, 3:4], lams[:, 2:3], ALU.subtract))
                            link(TT(lams[:, 5:6], lams[:, 4:5], lconst[:, 0:1], ALU.subtract))
                        elif what == "vt":
                            t = it[1]
                            kind, n, s = tiles[t]
                            dst = v_b[:, :, P * (kind == "vwb"):P * (kind == "vwb") + P] if kind[0:2] in ("vs", "vw") else v_ac[:, :, n * P:(n + 1) * P]
                            dve.wait_ge(M["pe_misc"], misc.after(it))
                            if kind == "vc" and n == 0:
                                dve.wait_ge(M["pe_v"], last_prob[(3, NQ - 1)] + 1)
                            dve.tensor_copy(dst, Mb[:].rearrange("p (i c) -> p i c", i=NQ)).then_inc(M["dve_misc"], 1)
                        elif what == "kcmp":
                            dve.wait_ge(M["pe_misc"], misc.after(it))
                            for g in range(2):
                                ps = slice(HD * g, HD * g + HD)
                                ins = TS(kcmpT[ps, C32 * g:C32 * g + C32], Mb[ps, C32 * g:C32 * g + C32], 0.5, None, ALU.mult)
                            ins.then_inc(M["dve_misc"], 1)
                        elif what == "vcmp":
                            dve.wait_ge(M["pe_misc"], misc.after(it))
                            for q in range(4):
                                ps, cs = slice(32 * q, 32 * q + 32), slice(HD * (q % 2), HD * (q % 2) + HD)
                                ins = TS(vbd[ps, cs], Mb[ps, cs], 0.5, None, ALU.mult)
                            ins.then_inc(M["dve_misc"], 1)
                        elif what == "rot":
                            t = it[1]
                            hi_, lo_, u = rot_dst(*tiles[t][:2])
                            r = rots.after(t)
                            dve.wait_ge(M["pool_rot"], r)
                            dve.wait_ge(M["dve_rm"], r)
                            TT(rc[:], rc[:], rb[:], ALU.add).then_inc(M["dve_rs"], 1)
                            dve.wait_ge(M["act_rot"], r)
                            TT(lo_, rc[:], f(hi_), ALU.subtract).then_inc(M["qk_s"], 1)
                        elif what == "S":
                            r = it[1]
                            n = (rows[r][1] + 1) * P
                            dve.wait_ge(M["pe_s"], r + 1)
                            if r >= 8:
                                dve.wait_ge(M["act_exp"], r - 7)
                            RED(nmax[:, r % 8:r % 8 + 1], Sc[r % 2][:, 0:n], AX.X, ALU.max, negate=True).then_inc(M["dve_max"], 1)
                        elif what == "T" and it[1] in pt_dve.order:
                            copy_pt(dve, it[1])
                        elif what == "CB":
                            r = it[1]
                            u, i, _, _ = rows[r]
                            n, b = (i + 1) * P, u % 2
                            p0, p1 = probs[:, (r - 1) % NP_, 0:n], probs[:, r % NP_, 0:n]
                            dve.wait_ge(M["act_exp"], r + 1)
                            link(dve.reciprocal(coef[:, b, 0:2], sums[:, b, i, 0:2]))
                            link(TT(coef[:, b, 2:3], coef[:, b, 1:2], lams[:, 5:6], ALU.mult))
                            link(TS(p0, p0, coef[:, b, 0:1], None, ALU.mult))
                            STT(p0, p1, coef[:, b, 2:3], p0, ALU.mult, ALU.add).then_inc(M["dve_comb"], 1)
                        elif what == "cs":
                            u = it[1]
                            dve.wait_ge(M["pe_misc"], misc.after(it))
                            if u > 4:
                                dve.wait_ge(M["act_cx"], u - 4)
                            TT(cs_[:], Mb[:, 0:2 * NQ * C32].rearrange("p (i h c) -> p i h c", i=NQ, h=2),
                               cmask[:].unsqueeze(2).to_broadcast([P, NQ, 2, C32]), ALU.add).then_inc(M["dve_misc"], 1)
                            dve.wait_ge(M["dve_misc"], misc.after(it))
                            link(RED(cmx[:], cs_[:].rearrange("p i h c -> p (i h) c"), AX.X, ALU.max))
                            TT(cs_[:].rearrange("p i h c -> p (i h) c"), cs_[:].rearrange("p i h c -> p (i h) c"),
                               cmx[:].unsqueeze(2).to_broadcast([P, 2 * NQ, C32]), ALU.subtract).then_inc(M["cs_s"], 1)
                        elif what == "cx":
                            u = it[1]
                            dve.wait_ge(M["act_cx"], u - 3)
                            link(RED(sums[:, u % 2, :, 0:2], pc[:], AX.X, ALU.add))
                            for h in range(2):
                                ins = STT(pc[:, :, h, :], cmask[:], 0.0, pc[:, :, h, :], ALU.is_equal, ALU.mult)
                            ins.then_inc(M["cprob_s"], 1)
                        elif what == "ct":
                            u = it[1]
                            dve.wait_ge(M["pe_misc"], misc.after(it))
                            if u > 4:
                                dve.wait_ge(M["pe_v"], last_prob[(u - 1, NQ - 1)] + 1)
                            dve.tensor_copy(pcT[:], Mb[:, 0:2 * P].rearrange("p (g q) -> p g q", g=2)).then_inc(M["dve_misc"], 1)
                        elif what == "N":
                            u, i = divmod(it[1], NQ)
                            b = u % 2
                            dve.wait_ge(M["pe_v"], last_prob[(u, i)] + 1)
                            if u and i == 0:
                                dve.wait_ge(M["pe_misc"], misc.after(("Y", u - 1)))
                            if branch(u) == "A":
                                link(dve.reciprocal(coef[:, b, 0:2], sums[:, b, i, 0:2]))
                                TT(y_q[:, i, :].rearrange("p (h d) -> p h d", h=2), Ob[:, 0:P].rearrange("p (h d) -> p h d", h=2),
                                   coef[:, b, 0:2].unsqueeze(2).to_broadcast([P, 2, HD]), ALU.mult).then_inc(M["dve_norm_o"], 1)
                            elif branch(u) == "B":
                                link(dve.reciprocal(coef[:, b, 0:6], sums[:, b, i, 0:6]))
                                gv = gates[:, i, :].rearrange("p (g n b) -> p b g n", g=2, n=4)[:, :, :, u - 4]
                                link(TT(coef[:, b, 0:6].rearrange("p (b h) -> p b h", b=3),
                                        coef[:, b, 0:6].rearrange("p (b h) -> p b h", b=3), gv, ALU.mult))
                                TT(tmp[:].rearrange("p (b d) -> p b d", b=6), Ob[:, 0:384].rearrange("p (b d) -> p b d", b=6),
                                   coef[:, b, 0:6].unsqueeze(2).to_broadcast([P, 6, HD]), ALU.mult).then_inc(M["dve_norm_o"], 1)
                                dve.wait_ge(M["dve_norm_o"], it[1] + 1)
                                RED(y_q[:, i, :], tmp[:].rearrange("p (b f) -> p f b", b=3), AX.X, ALU.add).then_inc(M["yq_s"], 1)
                                dve.wait_ge(M["yq_s"], it[1] + 1 - 4 * NQ)
                            else:
                                dve.tensor_copy(y_q[:, i, :], Ob[:, 0:P]).then_inc(M["dve_norm_o"], 1)
                        elif what == "MS":
                            u = it[1]
                            dve.wait_ge(M["act_msq"], NQ * (u - 7))
                            TS(msq[:, 1, :], msq[:, 0, :], 1.0 / P, EPS, ALU.mult, ALU.add).then_inc(M["ms_s"], 1)
                        elif what == "Y":
                            u = it[1]
                            if branch(u) == "C":
                                dve.wait_ge(M["pool_pow"], u - 7)
                                link(TT(msq[:, 3, :], msq[:, 2, :], msq[:, 2, :], ALU.mult))
                                link(TT(msq[:, 3, :], msq[:, 3, :], msq[:, 1, :], ALU.mult))
                                link(TS(msq[:, 3, :], msq[:, 3, :], -0.5, 1.5, ALU.mult, ALU.add))
                                link(TT(msq[:, 3, :], msq[:, 3, :], msq[:, 2, :], ALU.mult))
                                TT(y_q[:], y_q[:], msq[:, 3, :].unsqueeze(2).to_broadcast([P, NQ, P]),
                                   ALU.mult).then_inc(M["yqc_s"], 1)
                            dve.wait_ge(M["pe_misc"], misc.after(it))
                            if u >= 4:
                                dve.wait_ge(M["dve_ysplit"], ysplit.after(u - 4))
                            z = tile_of[("z" + branch(u).lower(), u % 4)]
                            dve.wait_ge(M["dve_evac"], dve_evac.after(z))
                            STT(y_f[:, y_slot(u), :], Mb[:], gsc[:, 0:1] if branch(u) == "C" else 0.5, zs[:],
                                ALU.mult, ALU.mult).then_inc(M["dve_misc"], 1)
                        elif what == "YS":
                            u = it[1]
                            dve.wait_ge(M["act_ys"], ysplit.after(u))
                            TT(y_lo[:, u % 4, :], y_f[:, y_slot(u), :], f(y_hi[:, u % 4, :]), ALU.subtract).then_inc(M["dve_ysplit"], 1)

                    with dve.Fori(0, NM // 2) as i:
                        for j in range(4):
                            t = T0 + j
                            lo(t + 2, i)
                            if j % 2:
                                m = i * 2 + j // 2
                                dve.wait_ge(M["act_evac"], i * 2 + (AE0 + j // 2 + 1))
                                dve.wait_ge(M["pe_dense"], i * 4 + (t + 1))
                                dve.wait_ge(M["dve_acc"], i * 2 + (DA0 + j // 2))
                                STT(rt[:], th[:, j // 2, :], 1.0, Dn[t % 2][:], ALU.add, ALU.mult).then_inc(M["dve_evac"], 1)
                                dve.wait_ge(M["dve_evac"], i * 2 + (DE0 + j // 2 + 1))
                                am = acc[:, bass.ds(m, 1), :].rearrange("p a s -> p (a s)")
                                TT(am, am, rt[:], ALU.add).then_inc(M["dve_acc"], 1)
                    for m in range(NM):
                        dve.wait_ge(M["act_merge"], m + 1)
                        STT(h_lo[:, m, :], acc[:, m, :], 0.5, f(h_hi[:, m, :]), ALU.mult, ALU.subtract).then_inc(M["dve_merge"], 1)
                    for c, b in ((0, Mb), (1, Ob)):
                        dve.wait_ge(M["act_p"], c + 1)
                        TT(y_lo[:, c, :], b[:], f(y_hi[:, c, :]), ALU.subtract).then_inc(M["dve_p"], 1)
                    with dve.Fori(0, NM // 4) as i:
                        for j in range(4):
                            t = T1 + j
                            xm = xT[:, bass.ds(i * 4 + j, 1), :].rearrange("p a s -> p (a s)")
                            lo(t + 2, i)
                            dve.wait_ge(M["pe_dense"], i * 4 + (t + 1))
                            TT(xm, Dn[t % 2][:], xm, ALU.add).then_inc(M["dve_evac"], 1)
                            dve.wait_ge(M["act_x1"], i * 4 + (j + 1))
                            TT(x1_lo[:, bass.ds(i * 4 + j, 1), :].rearrange("p a s -> p (a s)"), xm,
                               f(x1_hi)[:, bass.ds(i * 4 + j, 1), :].rearrange("p a s -> p (a s)"),
                               ALU.subtract).then_inc(M["x1_s"], 1)

                    def gate_tiles(i, m0, ahead):
                        for j in range(4):
                            t = T2 + 2 * m0 + j
                            if ahead or j < 2:
                                lo(t + 2, i, kt(("gate", "ple")[j % 2]))
                            if j % 2:
                                xm = xT[:, bass.ds(i * 2 + (m0 + j // 2), 1), :].rearrange("p a s -> p (a s)")
                                dve.wait_ge(M["act_evac"], i * 2 + (AE1 + m0 + j // 2 + 1))
                                dve.wait_ge(M["pe_dense"], i * 4 + (t + 1))
                                STT(rt[:], th[:, j // 2, :], 1.0, Dn[t % 2][:], ALU.add, ALU.mult).then_inc(M["dve_evac"], 1)
                                dve.wait_ge(M["dve_evac"], i * 2 + (DE2 + m0 + j // 2 + 1))
                                STT(xm, rt[:], 0.5, xm, ALU.mult, ALU.add).then_inc(M["dve_x"], 1)
                    with dve.Fori(0, NM // 2 - 1) as i:
                        gate_tiles(i, 0, True)
                    gate_tiles(0, NM - 2, False)

            for s_ in layer_sems:
                nc.gpsimd.sem_clear(s_)
            nc.all_engine_barrier()

        o_pe, o_act, o_dve, o_t, o_c, o_st = (sem(n) for n in ("o_pe", "o_act", "o_dve", "o_t", "o_c", "o_st"))
        with nc.Block() as block:
            @block.tensor
            def _(pe):
                pe.matmul(Mb[:], ones[:], ssum[:], start=True, stop=True).then_inc(o_pe, 1)
                for m in range(NM):
                    pe.wait_ge(o_dve, 5 + m + 1)
                    if m >= 2:
                        pe.wait_ge(o_c, m - 1)
                    for i in range(NQ):
                        ins = pe.transpose(Dn[m % 2][:, i * P:(i + 1) * P], th[:, m % 2, i * P:(i + 1) * P], ident[:])
                    ins.then_inc(o_t, 1)

            @block.scalar
            def _(act):
                act.wait_ge(o_dve, 1)
                act.activation(rx[:], rb[:], ACT.Ln).then_inc(o_act, 1)
                act.wait_ge(o_act, 1)
                act.activation(rs[:], rx[:], ACT.Exp, scale=-0.5).then_inc(o_act, 1)
                for m in range(NM):
                    act.wait_ge(o_t, m + 1)
                    act.activation(x_tok[:, :, m * P:(m + 1) * P], Dn[m % 2][:].rearrange("p (i c) -> p i c", i=NQ),
                                   ACT.Copy).then_inc(o_c, 1)

            @block.vector
            def _(dve):
                dve.wait_ge(o_pe, 1)
                dve.tensor_scalar(rb[:], Mb[:], 1.0 / D, EPS, ALU.mult, ALU.add).then_inc(o_dve, 1)
                dve.wait_ge(o_act, 2)
                dve.tensor_tensor(rc[:], rs[:], rs[:], ALU.mult).then_inc(o_dve, 1)
                dve.wait_ge(o_dve, 2)
                dve.tensor_tensor(rc[:], rc[:], rb[:], ALU.mult).then_inc(o_dve, 1)
                dve.wait_ge(o_dve, 3)
                dve.tensor_scalar(rc[:], rc[:], -0.5, 1.5, ALU.mult, ALU.add).then_inc(o_dve, 1)
                dve.wait_ge(o_dve, 4)
                dve.tensor_tensor(rs[:], rs[:], rc[:], ALU.mult).then_inc(o_dve, 1)
                dve.wait_ge(o_dve, 5)
                for m in range(NM):
                    if m >= 2:
                        dve.wait_ge(o_t, m - 1)
                    dve.scalar_tensor_tensor(th[:, m % 2, :], xT[:, m, :], finp[:, m:m + 1], rs[:],
                                             ALU.mult, ALU.mult).then_inc(o_dve, 1)

            @block.sync
            def _(sp):
                half = NM // 2
                for c in range(2):
                    sp.wait_ge(o_c, half * (c + 1))
                    cols = slice(c * half * P, (c + 1) * half * P)
                    sp.dma_start(out.rearrange("a (t p) d -> p (a t) d", p=P)[:, :, cols], x_tok[:, :, cols]).then_inc(o_st, 16)
                sp.wait_ge(o_st, 32)


_INS = ["x", "p", "positions", "norm_g", "w_in", "b_forget", "cmp_pe_k", "cmp_w1_k", "cmp_b1_k", "cmp_w2_k",
        "cmp_pe_v", "cmp_w1_v", "cmp_b1_v", "cmp_w2_v", "diff_lam", "diff_subln_g",
        "w_br_a", "w_br_b", "w_br_c", "w_out", "w_ple", "w_ple_gate", "final_g"]


def kernel(**inputs):
    import numpy as _np
    import concourse.bacc as _bacc
    from concourse import mybir as _mybir
    from concourse.bass_utils import run_bass_kernel_spmd as _run

    nc = _bacc.Bacc("TRN2", target_bir_lowering=False, num_devices=1)
    depth = inputs["norm_g"].shape[0]
    half = HD // 2
    freq = _np.float32(ROPE_THETA) ** (-_np.arange(half, dtype=_np.float32) / _np.float32(half))
    rope_consts = _np.stack([_np.tile(freq, P // half), _np.tile(_np.repeat([-1.0, 1.0], half), P // HD)], 1)
    lam0 = _np.array([0.8 - 0.6 * _np.exp(-0.3 * i) for i in range(depth)])
    layer_consts = _np.tile(_np.stack([lam0, 0.5 * (1.0 - lam0)], 1)[:, None, :], (1, P, 1))
    arrays, args = {}, []
    for name in _INS + ["rope_consts", "layer_consts"]:
        a = {"rope_consts": rope_consts, "layer_consts": layer_consts}.get(name)
        a = _np.ascontiguousarray(inputs[name] if a is None else a.astype(_np.float32))
        arrays[f"in_{name}_dram"] = a
        args.append(nc.dram_tensor(f"in_{name}_dram", a.shape, _mybir.dt.from_np(a.dtype), kind="ExternalInput").ap())
    args.append(nc.dram_tensor("out_dram", inputs["x"].shape, F32, kind="ExternalOutput").ap())
    hybrid_trunk(nc, *args)
    r = _run(nc, [arrays], core_ids=[0])
    return r.results[0]["out_dram"]
```

```python
from contextlib import ExitStack

import numpy as np

import concourse.bass as bass
from concourse import mybir

ALU = mybir.AluOpType
ACT = mybir.ActivationFunctionType
AX = mybir.AxisListType
F32 = mybir.dt.float32
F32R = mybir.dt.float32r
BF16 = mybir.dt.bfloat16
I32 = mybir.dt.int32

P = 128
HD = 64
EPS = 1e-6
NEG = -1e30
ROPE_THETA = 10000.0

COL = {}
_at = 0
for _name, _n in (("qa", 512), ("ka", 512), ("va", 512), ("fa", 8), ("za", 512),
                  ("qb", 512), ("kcb", 128), ("vcb", 128), ("ksb", 128), ("vsb", 128), ("kwb", 128), ("vwb", 128),
                  ("gb", 24), ("zb", 512), ("qc", 512), ("kc", 512), ("vc", 512), ("zc", 512), ("mg", 3072)):
    COL[_name] = _at
    _at += _n

RAW = 4
SPL = 2
NP_ = 4
UNITS = 12


def y_slot(u):
    return 0 if u < 4 else u % 4


def branch(u):
    return "ABC"[u // 4]



def dense_tiles():
    st = {-1: [("va", 0), ("fg", 0), ("qa", 0), ("ka", 0), ("va", 1)]}
    st[0] = [("qa", 1), ("ka", 1), ("za", 0), ("va", 2), ("kcb", 0)]
    st[1] = [("qa", 2), ("ka", 2), ("w1k", 0), ("ksb", 0), ("w1k", 1), ("za", 1), ("va", 3)]
    st[2] = [("qa", 3), ("w1k", 2), ("ka", 3), ("w1k", 3), ("za", 2), ("vcb", 0)]
    st[3] = [("qb", 0), ("w1v", 0), ("kwb", 0), ("w1v", 1), ("za", 3), ("w1v", 2), ("vsb", 0), ("w1v", 3), ("vwb", 0)]
    st[4] = [("qb", 1), ("vc", 0), ("zb", 0), ("mga", 0), ("bra", 0), ("mga", 1), ("bra", 1)]
    st[5] = [("qb", 2), ("vc", 1), ("zb", 1), ("mga", 2), ("bra", 2), ("mga", 3), ("bra", 3)]
    st[6] = [("qb", 3), ("vc", 2), ("zb", 2), ("vc", 3), ("mga", 4), ("bra", 4), ("mga", 5), ("bra", 5)]
    st[7] = [("qc", 0), ("zb", 3), ("kc", 0), ("mga", 6), ("bra", 6), ("mga", 7), ("bra", 7)]
    st[8] = [("qc", 1), ("mgb", 0), ("kc", 1), ("zc", 0), ("brb", 0), ("mgb", 1), ("brb", 1)]
    st[9] = [("qc", 2), ("mgb", 2), ("kc", 2), ("zc", 1), ("brb", 2), ("mgb", 3), ("brb", 3)]
    st[10] = [("qc", 3), ("mgb", 4), ("kc", 3), ("zc", 2), ("brb", 4), ("mgb", 5), ("brb", 5)]
    st[11] = [("mgb", 6), ("brb", 6), ("mgb", 7), ("brb", 7), ("zc", 3)]
    return st


KT = {"bra": 4, "brb": 4, "brc": 4, "ple": 2}
ROTATED = ("qb", "ksb", "kwb", "qc", "kc")
VALUES = ("va", "vsb", "vwb", "vc")
ACT_EVAC = ("qa", "ka", "za", "zb", "zc", "fg") + ROTATED + VALUES + ("mga", "mgb", "mgc", "gate")
DVE_EVAC = ("qa", "ka", "za", "zb", "zc", "fg", "kcb", "vcb", "w1k", "w1v", "bra", "brb", "brc", "out", "ple")


def kt(kind):
    return KT.get(kind, 8)


def steps(kind):
    return 4 if kind in ("w1k", "w1v") else kt(kind)


def evac_first(tiles, t):
    return tiles[t][0] in ROTATED + VALUES and t + 1 < len(tiles) and kt(tiles[t + 1][0]) == 8 \
        and tiles[t + 1][0] not in ("w1k", "w1v")


class Count:

    def __init__(self):
        self.order = {}

    def add(self, key):
        assert key not in self.order, key
        self.order[key] = len(self.order) + 1

    def after(self, key):
        return self.order[key]

    def __len__(self):
        return len(self.order)


def make_schedule(NQ):
    stages = dense_tiles()
    tiles = []
    for s in sorted(stages):
        tiles += [(kind, n, s) for kind, n in stages[s]]

    rows, prob_rows = [], []
    for u in range(UNITS):
        for i in range(NQ):
            if branch(u) == "A":
                maps = [("a", 0), ("a", 1)]
            elif branch(u) == "B":
                maps = [("sel", 0), ("sel", 1), ("win", 0), ("win", 1)]
            else:
                maps = [("c", 0), ("c", 1)]
            r0 = len(rows)
            rows += [(u, i, m, h) for m, h in maps]
            if branch(u) == "C":
                prob_rows.append((u, i, "c", 0, r0 + 1, True))
            else:
                for j, (m, h) in enumerate(maps):
                    prob_rows.append((u, i, m, h, r0 + j, j == len(maps) - 1))

    items = []
    follow = []

    def step_follow():
        for f in follow:
            f[0] -= 1
        while follow and follow[0][0] <= 0:
            items.append(follow.pop(0)[1])

    def dense_groups(s):
        for t in [t for t, x in enumerate(tiles) if x[2] == s]:
            for k in range(steps(tiles[t][0])):
                yield t, k

    def emit_group(g):
        t, k = g
        items.append(("mm", t, k))
        kind = tiles[t][0]
        step_follow()
        if k == steps(kind) - 1:
            items.append(("end", t))
            if kind in ROTATED:
                follow.append([8, ("swap", t)])
                follow.append([11, ("rot", t)])
            if kind in VALUES:
                follow.append([5, ("vt", t)])
            if kind == "fg":
                follow.extend([[3, ("lf1", t)], [7, ("gates", t)], [9, ("lf2", t)]])
            if kind == "brb" and tiles[t][1] == 7:
                for u in range(8, 11):
                    follow.append([1 + u - 8, ("YS", u)])
            if kind == "w1k" and tiles[t][1] == 3:
                follow.extend([[4, ("ht", t)], [7, ("kcmp", t)]])
            if kind == "w1v" and tiles[t][1] == 3:
                follow.extend([[4, ("ht", t)], [7, ("vcmp", t)]])
            follow.sort(key=lambda f: f[0])

    for g in dense_groups(-1):
        emit_group(g)

    vq, late, newton, combs = [], [], [], []
    tick = 0
    ti = 0
    for s in range(UNITS):
        groups = list(dense_groups(s))
        rs = [r for r, x in enumerate(rows) if x[0] == s]
        tail = 7 if s == UNITS - 1 else 0
        N = len(rs) + tail
        G = len(groups)
        done = 0
        for j in range(N):
            parts = []
            if j < len(rs):
                r = rs[j]
                parts.append(("S", r))
            if j < len(rs) and branch(s) == "B" and j < 3:
                parts.append((("cs", "cx", "ct")[j], s))
            while combs and combs[0][0] <= tick:
                parts.append(combs.pop(0)[1])
            if j < len(rs) and branch(s) == "C" and rows[rs[j]][3] == 1:
                combs.append((tick + 1, ("CB", rs[j])))
            if ti < len(prob_rows):
                lag = 2 if branch(prob_rows[ti][0]) == "C" else 1
                limit = tick - lag
                while ti < len(prob_rows) and prob_rows[ti][4] <= limit:
                    parts.append(("T", ti))
                    vq.append((tick + 1, ti))
                    ti += 1
            while late and late[0][0] <= tick:
                parts.append(late.pop(0)[1])
            while vq and vq[0][0] <= tick:
                k = vq.pop(0)[1]
                parts.append(("V", k))
                if prob_rows[k][5]:
                    u, i = prob_rows[k][:2]
                    parts.append(("N", NQ * u + i))
                    if i == NQ - 1:
                        if branch(u) == "C":
                            late.append((tick + 1, ("MS", u)))
                            newton.append((tick + 1, ("YN", u)))
                            if u < UNITS - 1:
                                late.append((tick + 2, ("Y", u)))
                        else:
                            late.append((tick + 1, ("Y", u)))
            while newton and newton[0][0] <= tick:
                parts.append(newton.pop(0)[1])
            if s == 8 and 1 <= j <= 4:
                parts.append(("YS", 3 + j))
            want = (j + 1) * G // N
            n = want - done
            for m, part in enumerate(parts):
                items.append(part)
                if part[0] == "N" and branch(part[1] // NQ) == "C":
                    follow.append([1, ("SQ", part[1])])
                    follow.sort(key=lambda f: f[0])
                if part[0] == "Y" and branch(part[1]) == "A":
                    items.append(("YS", part[1]))
                share = (m + 1) * n // len(parts) - m * n // len(parts)
                if m == len(parts) - 1:
                    share = want - done
                for _ in range(share):
                    emit_group(groups[done])
                    done += 1
            if not parts:
                while done < want:
                    emit_group(groups[done])
                    done += 1
            tick += 1
    while follow:
        items.append(follow.pop(0)[1])
    items += [("Y", UNITS - 1), ("YS", UNITS - 1)]
    assert not late and not newton and not vq and ti == len(prob_rows)
    where = {x: n for n, x in enumerate(items)}
    for u in range(8, UNITS):
        assert where[("SQ", NQ * u + NQ - 1)] < where[("MS", u)], u
    for u in range(1, UNITS):
        z = tiles.index(("z" + branch(u).lower(), u % 4, u))
        assert where[("end", z)] > where[("Y", u - 1)], u
        assert where[("end", z)] < where[("Y", u)], u
        assert where[("Y", u - 1)] < where[("N", NQ * u)], u
    return tiles, rows, prob_rows, items


def hybrid_trunk(nc, x, p, positions, norm_g, w_in, b_forget, cmp_pe_k, cmp_w1_k, cmp_b1_k, cmp_w2_k,
                 cmp_pe_v, cmp_w1_v, cmp_b1_v, cmp_w2_v, diff_lam, diff_subln_g,
                 w_br_a, w_br_b, w_br_c, w_out, w_ple, w_ple_gate, final_g, rope_consts, layer_consts, out):
    _, S, D = x.shape
    DEPTH = norm_g.shape[0]
    NQ = S // P
    NM = D // P
    CS, NC = 16, (S - 32) // 16 + 1
    C32 = 32
    QSCALE = HD ** -0.5
    HIDDEN = cmp_w1_k.shape[2]

    tiles, rows, prob_rows, items = make_schedule(NQ)
    T0 = len(tiles)
    T1 = T0 + 2 * NM
    T2 = T1 + NM
    T3 = T2 + 2 * NM
    assert NM % 4 == 0

    act_evac, dve_evac, rots, qk_ready, misc = Count(), Count(), Count(), Count(), Count()
    pt_act, pt_dve, ysplit, hids = Count(), Count(), Count(), Count()
    for it in items:
        if it[0] == "end":
            kind, n, _ = tiles[it[1]]
            if kind in ACT_EVAC:
                act_evac.add(it[1])
            if kind in DVE_EVAC:
                dve_evac.add(it[1])
            if kind in ROTATED:
                rots.add(it[1])
            if kind in ("w1k", "w1v") and n == 3:
                hids.add(kind)
        elif it[0] == "rot":
            qk_ready.add(tiles[it[1]][:2])
        elif it[0] in ("vt", "gates", "ht", "kcmp", "vcmp", "cs", "ct", "Y"):
            misc.add(it)
        elif it[0] == "T":
            (pt_act if it[1] % 2 and branch(prob_rows[it[1]][0]) == "B" else pt_dve).add(it[1])
        elif it[0] == "YS":
            ysplit.add(it[1])
    DA0 = NM
    rows_before = {}
    for r, x_ in enumerate(rows):
        rows_before.setdefault(x_[0], r)
    th_slot, n_th = {}, 0
    for t, (kind, n, _) in enumerate(tiles):
        if kind in ("fg", "za", "zb", "zc", "mga", "mgb"):
            th_slot[t] = n_th % 2
            n_th += 1
    AE0, DE0 = len(act_evac), len(dve_evac)
    AE1, DE1 = AE0 + NM, DE0 + NM
    DE2 = DE1 + NM
    EARLY = 6

    prob_of_row = {}
    for k, x_ in enumerate(prob_rows):
        prob_of_row[x_[4]] = k
        if x_[2] == "c":
            prob_of_row[x_[4] - 1] = k
    first_prob, last_prob = {}, {}
    for k, (u, i, *_r) in enumerate(prob_rows):
        first_prob.setdefault((u, i), k)
        last_prob[(u, i)] = k

    def w_cols(L, w, c0, n, k):
        return w[bass.ds(L, 1), 0:k * P, bass.ds(c0, n)].rearrange("a (k p) n -> p (a k) n", p=P)

    def sources(L, kind, n):
        full = lambda w, c0: [(slice(0, P), slice(0, P), w_cols(L, w, c0, P, kt(kind)))]
        if kind == "fg":
            return [(slice(0, P), slice(0, 32), w_cols(L, w_in, COL["fa"], 32, 8)),
                    (slice(0, P), slice(32, P), w_cols(L, w_in, COL["gb"], 96, 8))]
        if kind in ("qb", "zb"):
            return [(slice(0, P), slice(HD * g, HD * g + HD), w_cols(L, w_in, COL[kind] + 256 * g + HD * n, HD, 8))
                    for g in range(2)]
        if kind in ("w1k", "w1v"):
            w = cmp_w1_k if kind == "w1k" else cmp_w1_v
            src = w[bass.ds(L, 1), n * 512:(n + 1) * 512, :]
            return [(slice(0, P), slice(0, HIDDEN), src.rearrange("a (k p) n -> p (a k) n", p=P))]
        if kind in ("mga", "mgb", "mgc"):
            return full(w_in, COL["mg"] + D * "abc".index(kind[2]) + n * P)
        if kind == "brb":
            return [(slice(HD * g, HD * g + HD), slice(0, P),
                     w_br_b[bass.ds(L, 1), 256 * g:256 * g + 256, bass.ds(n * P, P)].rearrange(
                         "a (k p) n -> p (a k) n", p=HD)) for g in range(2)]
        if kind in ("bra", "brc"):
            return full(w_br_a if kind == "bra" else w_br_c, n * P)
        if kind == "out":
            return full(w_out, n * P)
        if kind == "gate":
            return full(w_ple_gate, n * P)
        if kind == "ple":
            return full(w_ple, n * P)
        return full(w_in, COL[kind] + n * P)

    landed, slot_sum = [], [0] * RAW
    for t, (kind, n, _) in enumerate(tiles):
        slot_sum[t % RAW] += 16 * (2 if kind in ("fg", "qb", "zb", "brb") else 1)
        landed.append(slot_sum[t % RAW])

    ctx = ExitStack()
    with ctx:
        def sb(name, shape, dt=F32):
            return ctx.enter_context(nc.sbuf_tensor(name, shape, dt))

        def bank(name):
            return ctx.enter_context(nc.psum_tensor(name, [P, 512], F32))

        sems = []

        def sem(name):
            s = ctx.enter_context(nc.semaphore(name))
            sems.append(s)
            return s

        xT = sb("xT", [P, NM, S])
        acc = sb("acc", [P, NM, S])
        h_hi = sb("h_hi", [P, NM, S], F32R)
        h_lo = sb("h_lo", [P, NM, S], F32R)
        raw = sb("raw", [P, RAW, 8 * P])
        w_hi = sb("w_hi", [P, SPL, 8 * P], F32R)
        w_lo = sb("w_lo", [P, SPL, 8 * P], F32R)
        arena = sb("arena", [P, 16 * S], F32R)

        def part(n, k=1):
            return arena[:, n * S:(n + k) * S]
        q_hi, q_lo = [part(0), part(1)], [part(2), part(3)]
        k_hi, k_lo = [part(4), part(5)], [part(6), part(7)]
        ks_hi, ks_lo, kw_hi, kw_lo = part(8), part(9), part(10), part(11)
        flat_hi = part(12, 2).rearrange("p (m c) -> p m c", m=16)
        flat_lo = part(14, 2).rearrange("p (m c) -> p m c", m=16)
        x1_hi = part(0, NM).rearrange("p (m s) -> p m s", m=NM)
        x1_lo = part(NM, NM).rearrange("p (m s) -> p m s", m=NM)
        y_hi = sb("y_hi", [P, 4, S], F32R)
        y_lo = sb("y_lo", [P, 4, S], F32R)
        y_f = sb("y_f", [P, 4, S])
        v_ac = sb("v_ac", [P, NQ, 512])
        v_b = sb("v_b", [P, NQ, 256])
        probs = sb("probs", [P, NP_, S])
        pT = sb("pT", [P, 2, S])
        zs = sb("zs", [P, S])
        th = sb("th", [P, 2, S])
        vT = y_f[:, 3, :]
        qf = sb("qf", [P, S])
        rx = sb("rx", [P, S])
        rs = sb("rs", [P, S])
        rb = sb("rb", [P, S])
        rc = sb("rc", [P, S])
        flat = v_b[:].rearrange("p i c -> p (i c)").rearrange("p (m c) -> p m c", m=16)
        cosT = sb("cosT", [P, S])
        sinT = sb("sinT", [P, S])
        ssum = zs
        ident = sb("ident", [P, P])
        ones = sb("ones", [P, P])
        identb = sb("identb", [P, P], BF16)
        maskb = sb("maskb", [P, P], BF16)
        cmask = sb("cmask", [P, NQ, C32])
        self_ = sb("self_", [P, 8])
        selr = sb("selr", [P, 8], F32R)
        ck = sb("ck", [P, S], F32R)
        par = sb("par", [P, 48])
        finp = sb("finp", [P, 8])
        w2k = y_f[:, 1, 128:384].rearrange("p (a c) -> p a c", a=2)
        w2v = y_f[:, 1, 384:512].rearrange("p (a c) -> p a c", a=2)
        bfor = sb("bfor", [8, 1])
        lconst = sb("lconst", [P, 2])
        rconst = sb("rconst", [P, 2])
        lams = sb("lams", [P, 8])
        gsc = sb("gsc", [P, 1])
        gates = sb("gates", [P, NQ, 24])
        lf = probs[0:8]
        hid = y_f[:, 2, :].rearrange("p (a g b c) -> p a g b c", a=2, g=2, b=4)
        kcmpT = sb("kcmpT", [P, 2 * C32])
        vbd = sb("vbd", [P, P])
        cs_ = sb("cs_", [P, NQ, 2, C32])
        pc = cs_
        pcT = sb("pcT", [P, 2, P])
        cmx = sb("cmx", [P, 2 * NQ])
        nmax = sb("nmax", [P, 8])
        sums = sb("sums", [P, 2, NQ, 6])
        coef = sb("coef", [P, 2, 8])
        y_q = sb("y_q", [P, NQ, P])
        prow = y_q[0:48, 0, :]
        tmp = sb("tmp", [P, 384])
        msq = sb("msq", [P, 4, NQ])
        halfs = sb("halfs", [P, NQ])
        sqj = cs_[:].rearrange("p i h c -> p (i h c)")[:, 0:P]
        lamr = tmp[:, 0:4 * HD]
        hacc = tmp[0:2 * C32, 0:HIDDEN]
        b1 = {"w1k": qf[0:2 * C32, 0:HIDDEN], "w1v": pcT[0:2 * C32].rearrange("p g q -> p (g q)")}
        hth = cs_[0:2 * C32].rearrange("p i h c -> p (i h c)")
        rt = qf
        posi = pT[:, 0, :].bitcast(I32)

        Dn = [bank("D0"), bank("D1")]
        Sc = [bank("S0"), bank("S1")]
        Tr = [bank("T0"), bank("T1")]
        Ob = bank("Ob")
        Mb = bank("Mb")

        def f(ap):
            return ap.bitcast(F32)

        i_ld, i_const, i_pe, i_dve, i_act = (sem(n) for n in ("i_ld", "i_const", "i_pe", "i_dve", "i_act"))
        i_fin, i_ang = sem("i_fin"), sem("i_ang")
        i_x = [sem("i_x0"), sem("i_x1")]
        ANGLE_STEPS = 11
        xsq = raw[:].rearrange("p r (c s) -> p (r c) s", s=S)
        x_tok = acc[:].rearrange("p m s -> p (m s)").rearrange("p (t d) -> p t d", t=NQ)
        with nc.Block() as block:
            @block.sync
            def _(sp):
                sp.dma_start(posi, positions.to_broadcast([P, S])).then_inc(i_ld, 16)
                sp.dma_start(rconst[:], rope_consts).then_inc(i_ld, 16)
                for h in range(2):
                    cols = slice(h * D // 2, (h + 1) * D // 2)
                    sp.dma_start(x_tok[:, :, cols], x.rearrange("a (t p) d -> p (a t) d", p=P)[:, :, cols]).then_inc(i_x[h], 16)
                sp.dma_start(prow[0:NM, :], final_g.rearrange("(m p) -> m p", p=P)).then_inc(i_fin, 16)

            @block.gpsimd
            def _(pool):
                pool.memset(ident[:], 0.0).then_inc(i_const, 1)
                pool.wait_ge(i_const, 1)
                pool.affine_select(out=ident[:], in_=ident[:], compare_op=ALU.not_equal, fill=1.0, base=0,
                                   pattern=[[-1, P]], channel_multiplier=1).then_inc(i_const, 1)
                pool.memset(ones[:], 1.0).then_inc(i_const, 1)
                pool.memset(maskb[:], 0.0).then_inc(i_const, 1)
                pool.memset(cmask[:], 0.0).then_inc(i_const, 1)
                pool.memset(self_[:], 0.0).then_inc(i_const, 1)
                pool.memset(halfs[:], -0.5).then_inc(i_const, 1)
                pool.memset(vbd[:], 0.0).then_inc(i_const, 1)
                pool.memset(kcmpT[:], 0.0).then_inc(i_const, 1)
                pool.memset(f(ck[:]), 0.0).then_inc(i_const, 1)
                pool.wait_ge(i_const, 10)
                pool.tensor_copy(identb[:], ident[:]).then_inc(i_const, 1)
                pool.affine_select(out=maskb[:], in_=maskb[:], compare_op=ALU.is_ge, fill=NEG, base=0,
                                   pattern=[[-1, P]], channel_multiplier=1).then_inc(i_const, 1)
                pool.affine_select(out=cmask[:], in_=cmask[:], compare_op=ALU.is_ge, fill=NEG, base=-31,
                                   pattern=[[P, NQ], [-CS, C32]], channel_multiplier=1).then_inc(i_const, 1)
                for n, r in enumerate((0, 32)):
                    pool.affine_select(out=self_[:], in_=self_[:], compare_op=ALU.not_equal, fill=1.0, base=-r,
                                       pattern=[[-1, 8]], channel_multiplier=1).then_inc(i_const, 1)
                    pool.wait_ge(i_const, 14 + n)
                pool.tensor_copy(selr[:], self_[:]).then_inc(i_const, 1)

            NB = NM

            @block.tensor
            def _(pe):
                pe.wait_ge(i_const, 2)
                for m in range(NB):
                    if m in (0, NB // 2):
                        pe.wait_ge(i_x[m // (NB // 2)], 16)
                    if m >= 2:
                        pe.wait_ge(i_dve, m - 1)
                    for t in range(NQ):
                        ins = pe.transpose(Dn[m % 2][:, t * P:(t + 1) * P], x_tok[:, t, m * P:(m + 1) * P], ident[:])
                    ins.then_inc(i_pe, 1)
                pe.wait_ge(i_fin, 16)
                pe.transpose(Mb[:, 0:NM], prow[0:NM, :], ident[0:NM, 0:NM]).then_inc(i_pe, 1)

            @block.vector
            def _(dve):
                n = 0

                def link(ins):
                    nonlocal n
                    n += 1
                    ins.then_inc(i_ang, 1)
                    dve.wait_ge(i_ang, n)
                dve.wait_ge(i_ld, 32)
                link(dve.tensor_copy(rx[:], posi))
                link(dve.tensor_scalar(rx[:], rx[:], rconst[:, 0:1], None, ALU.mult))
                MAGIC = 12582912.0
                link(dve.tensor_scalar(rs[:], rx[:], 1.0 / (2 * np.pi), MAGIC, ALU.mult, ALU.add))
                link(dve.tensor_scalar(rs[:], rs[:], MAGIC, None, ALU.subtract))
                c1 = 6.28125
                c2 = float(np.float32(np.round((2 * np.pi - c1) * 2 ** 20) / 2 ** 20))
                c3 = 2 * np.pi - c1 - c2
                for c in (c1, c2, c3):
                    link(dve.scalar_tensor_tensor(rx[:], rs[:], -c, rx[:], ALU.mult, ALU.add))
                link(dve.tensor_scalar(rx[:], rx[:], -3.1415925, 3.1415925, ALU.max, ALU.min))
                link(dve.tensor_scalar(rb[:], rx[:], -1.0, None, ALU.mult))
                link(dve.tensor_tensor(rb[:], rb[:], rx[:], ALU.max))
                link(dve.tensor_scalar(rb[:], rb[:], -1.0, float(np.pi / 2), ALU.mult, ALU.add))
                for m in range(NB + 2):
                    if m < NB:
                        dve.wait_ge(i_pe, m + 1)
                        dve.tensor_copy(xT[:, m, :], Dn[m % 2][:]).then_inc(i_dve, 1)
                    if m >= 2:
                        dve.wait_ge(i_act, m + 1)
                        if m == 2:
                            link(dve.tensor_copy(ssum[:], xsq[:, 0, :]))
                        else:
                            link(dve.tensor_tensor(ssum[:], ssum[:], xsq[:, m - 2, :], ALU.add))
                dve.wait_ge(i_act, 2)
                link(dve.tensor_scalar(sinT[:], rc[:], rconst[:, 1:2], None, ALU.mult))
                dve.wait_ge(i_pe, NB + 1)
                dve.tensor_copy(finp[:], Mb[:, 0:NM]).then_inc(i_dve, 1)


            @block.scalar
            def _(act):
                act.wait_ge(i_ang, ANGLE_STEPS)
                act.activation(cosT[:], rb[:], ACT.Sin).then_inc(i_act, 1)
                act.activation(rc[:], rx[:], ACT.Sin).then_inc(i_act, 1)
                for m in range(NM):
                    act.wait_ge(i_dve, m + 1)
                    act.activation(xsq[:, m, :], xT[:, m, :], ACT.Square).then_inc(i_act, 1)

        p_tok = y_f[:, 0:2, :].rearrange("p a s -> p (a s)").rearrange("p (t c) -> p t c", t=NQ)
        tile_of = {x_[:2]: t for t, x_ in enumerate(tiles)}
        names = ("par_ld par2_ld pe_par pe_norm act_norm dve_norm h_hi_s h_lo_s act_hi dve_lo pe_dense act_evac "
                 "dve_evac dve_chain sw_ld pool_rot dve_rm dve_rs act_rot qk_s pe_s dve_max act_exp dve_comb pe_t "
                 "pt_act_s pt_dve_s pe_v dve_norm_o yq_s yqc_s pe_misc dve_misc dve_ysplit act_ys dve_hid act_hid "
                 "lf_s act_lf lam_s act_lam ck_s cs_s act_cx cprob_s ms_s pool_pow act_msq act_merge dve_merge "
                 "zero_s act_x1 x1_s dve_acc dve_x act_sq pool_sum p_ld pe_p dve_p act_p flat_s act_flat").split()
        sems_before = len(sems)
        M = {n: sem(n) for n in names}
        raw_ld = [sem(f"raw_ld{j}") for j in range(RAW)]
        layer_sems = sems[sems_before:]

        def pt_wait(eng, k):
            if k in pt_act.order:
                eng.wait_ge(M["pt_act_s"], pt_act.after(k))
            else:
                eng.wait_ge(M["pt_dve_s"], pt_dve.after(k))

        def copy_pt(eng, k):
            n = (prob_rows[k][1] + 1) * P
            eng.wait_ge(M["pe_t"], k + 1)
            if k >= 2:
                eng.wait_ge(M["pe_v"], k - 1)
            if k in pt_act.order:
                eng.activation(pT[:, k % 2, 0:n], Tr[k % 2][:, 0:n], ACT.Copy).then_inc(M["pt_act_s"], 1)
            else:
                eng.tensor_copy(pT[:, k % 2, 0:n], Tr[k % 2][:, 0:n]).then_inc(M["pt_dve_s"], 1)

        def kind_of(t):
            if t < T0:
                return tiles[t][0]
            if t < T1:
                return ("mgc", "brc")[(t - T0) % 2]
            if t < T2:
                return "out"
            return ("gate", "ple")[(t - T2) % 2]

        def landed_at(t):
            if t < T0:
                return landed[t]
            return slot_sum[t % RAW] + 16 * ((t - T0) // RAW + 1)

        def rot_dst(kind, n):
            if kind == "ksb":
                return ks_hi, ks_lo, None
            if kind == "kwb":
                return kw_hi, kw_lo, None
            u = (4 if kind == "qb" else 8) + n
            return (k_hi[u % 2], k_lo[u % 2], u) if kind == "kc" else (q_hi[u % 2], q_lo[u % 2], u)

        with nc.Fori(0, DEPTH) as L:
            with nc.Block() as block:

                @block.sync
                def _(sp):
                    rows_ = [(norm_g[bass.ds(L, 1), :].rearrange("a (m p) -> (a m) p", p=P), 0, 8),
                             (cmp_pe_k[bass.ds(L, 1)].rearrange("a (m two) d -> (a m) (two d)", two=2), 8, 16),
                             (cmp_pe_v[bass.ds(L, 1)].rearrange("a (m two) d -> (a m) (two d)", two=2), 24, 16),
                             (diff_subln_g[bass.ds(L, 1), :], 40, 1)]
                    def load(L, kind, n, t):
                        for ps, cs, src in sources(L, kind, n):
                            width = HIDDEN if kind in ("w1k", "w1v") else P
                            dst = raw[ps, t % RAW, 0:kt(kind) * P].rearrange("p (k n) -> p k n", n=width)[:, :, cs]
                            sp.dma_start(dst, src).then_inc(raw_ld[t % RAW], 16)

                    def static_load(t):
                        if t >= RAW:
                            sp.wait_ge(M["dve_lo"], 2 * (t - RAW + 1))
                        if t < T0:
                            load(L, tiles[t][0], tiles[t][1], t)
                        else:
                            load(L, ("mgc", "brc")[(t - T0) % 2], (t - T0) // 2, t)
                    static_load(0)
                    for src, r, n in rows_:
                        sp.dma_start(prow[r:r + n, :], src).then_inc(M["par_ld"], 16)
                    static_load(1)
                    small = [(w2k[:, :, 0:HD], cmp_w2_k[bass.ds(L, 1)].rearrange("a (k p) n -> p (a k) n", p=P)),
                             (w2k[:, :, HD:P], cmp_w2_k[bass.ds(L, 1)].rearrange("a (k p) n -> p (a k) n", p=P)),
                             (w2v, cmp_w2_v[bass.ds(L, 1)].rearrange("a (k p) n -> p (a k) n", p=P)),
                             (b1["w1k"], cmp_b1_k[bass.ds(L, 1), :].to_broadcast([2 * C32, HIDDEN])),
                             (b1["w1v"], cmp_b1_v[bass.ds(L, 1), :].to_broadcast([2 * C32, HIDDEN])),
                             (bfor[:], b_forget[bass.ds(L, 1), :].rearrange("a h -> h a")),
                             (lamr, diff_lam[bass.ds(L, 1)].rearrange("a f d -> a (f d)").to_broadcast([P, 4 * HD])),
                             (lconst[:], layer_consts[bass.ds(L, 1)].rearrange("a p c -> (a p) c"))]
                    for dst, src in small:
                        sp.dma_start(dst, src).then_inc(M["par2_ld"], 16)
                    for t in range(2, 6):
                        static_load(t)
                    for it in items:
                        if it[0] == "end" and tiles[it[1]][0] in ROTATED:
                            n = rots.after(it[1])
                            src = qf if tiles[it[1]][0] == "qb" else rx
                            sp.wait_ge(M["act_evac"], act_evac.after(it[1]))
                            if n > 1:
                                sp.wait_ge(M["pool_rot"], n - 1)
                            for a, b in ((0, 32), (32, 0), (64, 96), (96, 64)):
                                sp.dma_start(rs[a:a + 32, :], src[b:b + 32, :]).then_inc(M["sw_ld"], 16)
                        if it[0] == "end" and it[1] + 6 < T0 + 4:
                            static_load(it[1] + 6)
                    sp.wait_ge(M["dve_ysplit"], 12)
                    sp.dma_start(p_tok, p[bass.ds(L, 1)].rearrange("a b (t p) c -> p (a b t) c", p=P)).then_inc(M["p_ld"], 16)
                    with sp.Fori(0, NM // 2 - 1) as i:
                        for j in range(4):
                            t = T0 + 4 + j
                            sp.wait_ge(M["dve_lo"], i * 8 + 2 * (t - RAW + 1))
                            load(L, ("mgc", "brc")[j % 2], i * 2 + (2 + j // 2), t)
                    with sp.Fori(0, NM // 4) as i:
                        for j in range(4):
                            t = T1 + j
                            sp.wait_ge(M["dve_lo"], i * 8 + 2 * (t - RAW + 1))
                            load(L, "out", i * 4 + j, t)
                    with sp.Fori(0, NM // 2) as i:
                        for j in range(4):
                            t = T2 + j
                            sp.wait_ge(M["dve_lo"], i * 8 + 2 * (t - RAW + 1))
                            load(L, ("gate", "ple")[j % 2], i * 2 + j // 2, t)

                @block.gpsimd
                def _(pool):
                    pool.memset(flat, 0.0).then_inc(M["zero_s"], 1)
                    for m in range(NM):
                        pool.wait_ge(M["h_hi_s"], m + 1)
                        pool.tensor_tensor(h_lo[:, m, :], th[:, m % 2, :], f(h_hi[:, m, :]),
                                           ALU.subtract).then_inc(M["h_lo_s"], 1)
                    for it in items:
                        if it[0] == "swap":
                            n = rots.after(it[1])
                            pool.wait_ge(M["sw_ld"], 64 * n)
                            if n > 1:
                                pool.wait_ge(M["dve_rs"], n - 1)
                            pool.tensor_tensor(rb[:], rs[:], sinT[:], ALU.mult).then_inc(M["pool_rot"], 1)
                        if it[0] == "MS":
                            pool.wait_ge(M["ms_s"], it[1] - 7)
                            pool.tensor_tensor(msq[:, 2, :], msq[:, 1, :], halfs[:], ALU.pow).then_inc(M["pool_pow"], 1)
                    pool.wait_ge(M["dve_merge"], 1)
                    pool.memset(ssum[:], 0.0).then_inc(M["pool_sum"], 1)
                    with pool.Fori(0, NM // 2) as i:
                        for j in range(2):
                            pool.wait_ge(M["act_sq"], i * 2 + (j + 1))
                            pool.wait_ge(M["pool_sum"], i * 2 + (j + 1))
                            pool.tensor_tensor(ssum[:], ssum[:], probs[:, j, :], ALU.add).then_inc(M["pool_sum"], 1)

                @block.tensor
                def _(pe):
                    pe.matmul(Mb[:], ones[:], ssum[:], start=True, stop=True).then_inc(M["pe_norm"], 1)
                    pe.wait_ge(M["par_ld"], 64)
                    pe.transpose(Ob[:, 0:41], prow[0:41, :], ident[0:41, 0:41]).then_inc(M["pe_par"], 1)

                    moving = {"bra": (y_hi, y_lo),
                              "brb": (y_hi, y_lo), "brc": (y_hi, y_lo), "ple": (y_hi, y_lo),
                              "out": (h_hi, h_lo), "gate": (x1_hi, x1_lo)}

                    def dense(kind, t, k):
                        hi, lo = moving.get(kind, (h_hi, h_lo))
                        cs = slice(k * P, (k + 1) * P)
                        o = Dn[t % 2][:]
                        sl = t % SPL
                        last = k == kt(kind) - 1
                        pe.matmul(o, w_hi[:, sl, cs], hi[:, k, :], start=(k == 0), stop=False)
                        pe.matmul(o, w_lo[:, sl, cs], hi[:, k, :], start=False, stop=False)
                        ins = pe.matmul(o, w_hi[:, sl, cs], lo[:, k, :], start=False, stop=last)
                        if last:
                            ins.then_inc(M["pe_dense"], 1)

                    def hidden(n, t, k):
                        cs = slice(k * HIDDEN, (k + 1) * HIDDEN)
                        o = Dn[t % 2][0:2 * C32, 0:HIDDEN]
                        sl, m, last = t % SPL, 4 * n + k, k == 3
                        pe.matmul(o, flat_hi[:, m, :], w_hi[:, sl, cs], start=(k == 0), stop=False)
                        pe.matmul(o, flat_lo[:, m, :], w_hi[:, sl, cs], start=False, stop=False)
                        ins = pe.matmul(o, flat_hi[:, m, :], w_lo[:, sl, cs], start=False, stop=last)
                        if last:
                            ins.then_inc(M["pe_dense"], 1)

                    def bank_free(t):
                        if t < 2:
                            return
                        kind = tiles[t - 2][0]
                        if kind in DVE_EVAC:
                            pe.wait_ge(M["dve_evac"], dve_evac.after(t - 2))
                        else:
                            pe.wait_ge(M["act_evac"], act_evac.after(t - 2))

                    def misc_free(it):
                        n = misc.after(it)
                        if n > 1:
                            pe.wait_ge(M["dve_misc"], n - 1)

                    for it in items:
                        what = it[0]
                        if what == "mm":
                            t, k = it[1:]
                            kind, n, _ = tiles[t]
                            if k in (0, steps(kind) // 2):
                                pe.wait_ge(M["dve_lo"], 2 * t + 1 + (k > 0))
                            if k == 0:
                                bank_free(t)
                                if kind in ("w1k", "w1v") and n == 0:
                                    pe.wait_ge(M["flat_s"], 1 if kind == "w1k" else 2)
                                if kind in ("bra", "brb") and n == 0:
                                    pe.wait_ge(M["dve_ysplit"], 4 if kind == "bra" else 8)
                            if t == 0:
                                pe.wait_ge(M["h_lo_s"], k + 1)
                            if kind in ("w1k", "w1v"):
                                hidden(n, t, k)
                            else:
                                dense(kind, t, k)
                        elif what == "gates":
                            misc_free(it)
                            pe.wait_ge(M["act_evac"], act_evac.after(it[1]))
                            for i in range(NQ):
                                ins = pe.transpose(Mb[:, i * P:(i + 1) * P], th[:, 0, i * P:(i + 1) * P], ident[:])
                            ins.then_inc(M["pe_misc"], 1)
                        elif what == "vt":
                            misc_free(it)
                            pe.wait_ge(M["act_evac"], act_evac.after(it[1]))
                            for i in range(NQ):
                                ins = pe.transpose(Mb[:, i * P:(i + 1) * P], vT[:, i * P:(i + 1) * P], ident[:])
                            ins.then_inc(M["pe_misc"], 1)
                        elif what == "ht":
                            misc_free(it)
                            pe.wait_ge(M["dve_hid"], hids.after(tiles[it[1]][0]))
                            for ht in range(2):
                                ins = pe.transpose(Mb[:, 2 * C32 * ht:2 * C32 * (ht + 1)], hacc[:, ht * P:(ht + 1) * P],
                                                   ident[0:2 * C32, 0:2 * C32])
                            ins.then_inc(M["pe_misc"], 1)
                        elif what == "kcmp":
                            misc_free(it)
                            pe.wait_ge(M["dve_misc"], misc.after(("ht", it[1])))
                            pe.wait_ge(M["par2_ld"], 128)
                            for ht in range(2):
                                ins = pe.matmul(Mb[:, 0:64], w2k[:, ht, :], hid[:, ht, :, 0, :], start=(ht == 0), stop=(ht == 1))
                            ins.then_inc(M["pe_misc"], 1)
                        elif what == "vcmp":
                            misc_free(it)
                            pe.wait_ge(M["dve_misc"], misc.after(("ht", it[1])))
                            for g in range(2):
                                for ht in range(2):
                                    ins = pe.matmul(Mb[:, HD * g:HD * g + HD], hid[:, ht, g].rearrange("p b c -> p (b c)"),
                                                    w2v[:, ht, :], start=(ht == 0), stop=(ht == 1))
                            ins.then_inc(M["pe_misc"], 1)
                        elif what == "cs":
                            u = it[1]
                            misc_free(it)
                            if u == 4:
                                pe.wait_ge(M["dve_misc"], misc.after(("kcmp", tile_of[("w1k", 3)])))
                                pe.wait_ge(M["dve_misc"], misc.after(("vcmp", tile_of[("w1v", 3)])))
                            pe.wait_ge(M["act_evac"], act_evac.after(tile_of[("qb", u - 4)]))
                            for i in range(NQ):
                                ins = pe.matmul(Mb[:, 2 * C32 * i:2 * C32 * (i + 1)], qf[:, i * P:(i + 1) * P], kcmpT[:],
                                                start=True, stop=True)
                            ins.then_inc(M["pe_misc"], 1)
                        elif what == "ct":
                            misc_free(it)
                            pe.wait_ge(M["cprob_s"], it[1] - 3)
                            for g in range(2):
                                ins = pe.transpose(Mb[:, g * P:(g + 1) * P],
                                                   pc[:, 2 * g:2 * g + 2].rearrange("p i h c -> p (i h c)"), ident[:])
                            ins.then_inc(M["pe_misc"], 1)
                        elif what == "S":
                            r = it[1]
                            u, i, m, h = rows[r]
                            b = u % 2
                            if i == 0 and h == 0:
                                if m == "a":
                                    pe.wait_ge(M["dve_evac"], dve_evac.after(tile_of[("ka", u)]))
                                    if u == 0:
                                        pe.wait_ge(M["ck_s"], 2)
                                elif m == "c":
                                    pe.wait_ge(M["qk_s"], qk_ready.after(("kc", u - 8)))
                                elif m == "sel":
                                    pe.wait_ge(M["qk_s"], qk_ready.after(("qb", u - 4)))
                            if r >= 2:
                                pe.wait_ge(M["act_exp"], r - 1)
                            ps = slice(HD * h, HD * h + HD)
                            ka, kb = {"a": (k_hi[b], k_lo[b]), "c": (k_hi[b], k_lo[b]),
                                      "sel": (ks_hi, ks_lo), "win": (kw_hi, kw_lo)}[m]
                            n = (i + 1) * P
                            o = Sc[r % 2][:, 0:n]
                            qs = slice(i * P, n)
                            pe.matmul(o, q_hi[b][ps, qs], ka[ps, 0:n], start=True, stop=False)
                            pe.matmul(o, q_lo[b][ps, qs], ka[ps, 0:n], start=False, stop=False)
                            pe.matmul(o, q_hi[b][ps, qs], kb[ps, 0:n], start=False, stop=False)
                            if m == "a":
                                hh = 2 * u + h
                                pe.matmul(o, selr[:, hh:hh + 1].to_broadcast([P, P]), ck[:, 0:n], start=False, stop=False)
                            pe.matmul(Sc[r % 2][:, qs], identb[:], maskb[:], start=False, stop=True).then_inc(M["pe_s"], 1)
                        elif what == "T":
                            k = it[1]
                            u, i, m, h, r, _ = prob_rows[k]
                            if m == "c":
                                pe.wait_ge(M["dve_comb"], NQ * (u - 8) + i + 1)
                            else:
                                pe.wait_ge(M["act_exp"], r + 1)
                            if k >= 2:
                                pt_wait(pe, k - 2)
                            src = probs[:, (r - 1 if m == "c" else r) % NP_, :]
                            for j in range(i + 1):
                                ins = pe.transpose(Tr[k % 2][:, j * P:(j + 1) * P], src[:, j * P:(j + 1) * P], ident[:])
                            ins.then_inc(M["pe_t"], 1)
                        elif what == "V":
                            k = it[1]
                            u, i, m, h, r, last = prob_rows[k]
                            pt_wait(pe, k)
                            o = NQ * u + i
                            if k == first_prob[(u, i)]:
                                if o:
                                    pe.wait_ge(M["dve_norm_o"], o)
                                if i == 0:
                                    lastv = {"A": ("va", u), "B": ("vwb", 0), "C": ("vc", u - 8)}[branch(u)]
                                    pe.wait_ge(M["dve_misc"], misc.after(("vt", tile_of[lastv])))
                            if m == "c":
                                oc, vs = slice(0, P), lambda j: v_ac[:, j, (u - 8) * P:(u - 7) * P]
                            elif m == "a":
                                oc, vs = slice(HD * h, HD * h + HD), lambda j: v_ac[:, j, (2 * u + h) * HD:(2 * u + h + 1) * HD]
                            else:
                                bi = 1 if m == "sel" else 2
                                c0 = (bi - 1) * P + HD * h
                                oc, vs = slice(bi * P + HD * h, bi * P + HD * h + HD), lambda j: v_b[:, j, c0:c0 + HD]
                            for j in range(i + 1):
                                ins = pe.matmul(Ob[:, oc], pT[:, k % 2, j * P:(j + 1) * P], vs(j), start=(j == 0), stop=(j == i))
                            if last and branch(u) == "B":
                                if i == 0:
                                    pe.wait_ge(M["dve_misc"], misc.after(("ct", u)))
                                hs = slice(64 * (i % 2), 64 * (i % 2) + 64)
                                ins = pe.matmul(Ob[:, 0:P], pcT[hs, i // 2, :], vbd[hs, :], start=True, stop=True)
                            ins.then_inc(M["pe_v"], 1)
                        elif what == "Y":
                            u = it[1]
                            misc_free(it)
                            if branch(u) == "C":
                                pe.wait_ge(M["yqc_s"], u - 7)
                            elif branch(u) == "B":
                                pe.wait_ge(M["yq_s"], NQ * (u - 3))
                            else:
                                pe.wait_ge(M["dve_norm_o"], NQ * (u + 1))
                            for i in range(NQ):
                                ins = pe.transpose(Mb[:, i * P:(i + 1) * P], y_q[:, i, :], ident[:])
                            ins.then_inc(M["pe_misc"], 1)

                    with pe.Fori(0, NM // 2) as i:
                        for j in range(4):
                            t = T0 + j
                            kind = ("mgc", "brc")[j % 2]
                            if kind == "mgc":
                                pe.wait_ge(M["act_evac"], i * 2 + (AE0 + j // 2))
                                if j == 0:
                                    pe.wait_ge(M["dve_evac"], dve_evac.after(T0 - 2))
                            else:
                                pe.wait_ge(M["dve_evac"], i * 2 + (DE0 + j // 2))
                                pe.wait_ge(M["dve_ysplit"], UNITS)
                            for k in range(kt(kind)):
                                if k in (0, kt(kind) // 2):
                                    pe.wait_ge(M["dve_lo"], i * 8 + (2 * t + 1 + (k > 0)))
                                dense(kind, t, k)
                    pe.wait_ge(M["p_ld"], 16)
                    for c, b in ((0, Mb), (1, Ob)):
                        for t in range(NQ):
                            ins = pe.transpose(b[:, t * P:(t + 1) * P], p_tok[:, t, c * P:(c + 1) * P], ident[:])
                        ins.then_inc(M["pe_p"], 1)
                    pe.wait_ge(M["act_evac"], AE1)
                    with pe.Fori(0, NM // 4) as i:
                        for j in range(4):
                            t = T1 + j
                            pe.wait_ge(M["dve_evac"], i * 4 + (DE1 + j - 1))
                            for k in range(NM):
                                if k in (0, NM // 2):
                                    pe.wait_ge(M["dve_lo"], i * 8 + (2 * t + 1 + (k > 0)))
                                if j == 0:
                                    pe.wait_ge(M["dve_merge"], k + 1)
                                dense("out", t, k)
                    pe.wait_ge(M["dve_p"], 2)
                    with pe.Fori(0, NM // 2) as i:
                        for j in range(4):
                            t = T2 + j
                            kind = ("gate", "ple")[j % 2]
                            if kind == "gate":
                                pe.wait_ge(M["act_evac"], i * 2 + (AE1 + j // 2))
                                if j == 0:
                                    pe.wait_ge(M["dve_evac"], i * 2 + (DE2 - 1))
                            else:
                                pe.wait_ge(M["dve_evac"], i * 2 + (DE2 + j // 2))
                            for k in range(kt(kind)):
                                if k in (0, kt(kind) // 2):
                                    pe.wait_ge(M["dve_lo"], i * 8 + (2 * t + 1 + (k > 0)))
                                if j == 0:
                                    pe.wait_ge(M["x1_s"], k + 1)
                                dense(kind, t, k)

                @block.scalar
                def _(act):
                    A = act.activation
                    def hi(t, i=None, k=8, parts=(0, 1)):
                        sl, n = t % SPL, (kt(kind_of(t)) if i is None else k) * P
                        if i is None:
                            act.wait_ge(raw_ld[t % RAW], landed_at(t))
                            if t >= SPL:
                                act.wait_ge(M["pe_dense"], t - SPL + 1)
                        else:
                            act.wait_ge(raw_ld[t % RAW], i * 16 + landed_at(t))
                            act.wait_ge(M["pe_dense"], i * 4 + (t - SPL + 1))
                        for h in parts:
                            half = slice(h * n // 2, (h + 1) * n // 2)
                            A(w_hi[:, sl, half], raw[:, t % RAW, half], ACT.Copy).then_inc(M["act_hi"], 1)

                    act.wait_ge(M["dve_norm"], 1)
                    A(rx[:], rb[:], ACT.Ln).then_inc(M["act_norm"], 1)
                    act.wait_ge(M["act_norm"], 1)
                    A(rs[:], rx[:], ACT.Exp, scale=-0.5).then_inc(M["act_norm"], 1)
                    hi(0)
                    for m in range(NM):
                        act.wait_ge(M["dve_norm"], 5 + m + 1)
                        A(h_hi[:, m, :], th[:, m % 2, :], ACT.Copy).then_inc(M["h_hi_s"], 1)
                        if m == NM // 2:
                            hi(1)
                    th_free = []
                    last_vt = None
                    for it in items:
                        what = it[0]
                        if what == "end":
                            t = it[1]
                            kind, n, s = tiles[t]
                            D = Dn[t % 2]
                            late_hi = evac_first(tiles, t)
                            if not late_hi:
                                hi(t + 2)
                            if kind in ACT_EVAC:
                                act.wait_ge(M["pe_dense"], t + 1)
                            if kind in ("fg", "za", "zb", "zc", "mga", "mgb"):
                                c = len(th_free)
                                if c == 0:
                                    act.wait_ge(M["h_lo_s"], NM)
                                if c >= 2:
                                    act.wait_ge(*th_free[c - 2])
                                if kind == "fg":
                                    th_free.append((M["pe_misc"], 1))
                                elif kind[0] == "z":
                                    th_free.append((M["dve_evac"], dve_evac.after(t)))
                                else:
                                    th_free.append((M["dve_evac"], dve_evac.after(tile_of[("br" + kind[2], n)])))
                                A(th[:, c % 2, :], D[:], ACT.Tanh, scale=0.5).then_inc(M["act_evac"], 1)
                            if kind in ("qa", "ka"):
                                if n >= 2:
                                    act.wait_ge(M["pe_s"], rows_before[n - 1])
                                dst = (q_hi if kind == "qa" else k_hi)[n % 2]
                                A(dst, D[:], ACT.Copy, scale=QSCALE if kind == "qa" else 1.0).then_inc(M["act_evac"], 1)
                            if kind in ROTATED:
                                r = rots.after(t)
                                if r > 1:
                                    act.wait_ge(M["sw_ld"], 64 * (r - 1))
                                    act.wait_ge(M["dve_rm"], r - 1)
                                if kind == "qb" and n:
                                    act.wait_ge(M["pe_misc"], misc.after(("cs", 3 + n)))
                                dst = qf if kind == "qb" else rx
                                A(dst[:], D[:], ACT.Copy, scale=QSCALE if kind[0] == "q" else 1.0).then_inc(M["act_evac"], 1)
                            if kind in VALUES:
                                if last_vt is not None:
                                    act.wait_ge(M["pe_misc"], misc.after(("vt", last_vt)))
                                last_vt = t
                                A(vT, D[:], ACT.Copy).then_inc(M["act_evac"], 1)
                            if kind in ("kcb", "vcb"):
                                c = 0 if kind == "kcb" else 1
                                act.wait_ge(M["dve_evac"], dve_evac.after(t))
                                if c:
                                    act.wait_ge(M["pe_dense"], tile_of[("w1k", 3)] + 1)
                                A(flat_hi, flat, ACT.Copy).then_inc(M["act_flat"], 1)
                            if kind in ("w1k", "w1v") and n == 3:
                                act.wait_ge(M["dve_evac"], dve_evac.after(t))
                                A(hth, hacc, ACT.Tanh, scale=0.5).then_inc(M["act_hid"], 1)
                            if late_hi:
                                hi(t + 2)
                        elif what == "lf1":
                            act.wait_ge(M["lf_s"], 1)
                            A(lf[:, 2, :], lf[:, 1, :], ACT.Exp, scale=-1.0).then_inc(M["act_lf"], 1)
                            act.wait_ge(M["act_lf"], 1)
                            A(lf[:, 3, :], lf[:, 2, :], ACT.Ln, bias=1.0).then_inc(M["act_lf"], 1)
                        elif what == "gates":
                            act.wait_ge(M["lam_s"], 1)
                            A(lams[:, 2:4], lams[:, 0:2], ACT.Exp).then_inc(M["act_lam"], 1)
                        elif what == "rot":
                            t = it[1]
                            kind, n, s = tiles[t]
                            hi_, lo_, u = rot_dst(kind, n)
                            act.wait_ge(M["dve_rs"], rots.after(t))
                            if u is not None and u >= 2:
                                act.wait_ge(M["pe_s"], rows_before[u - 1])
                            A(hi_, rc[:], ACT.Copy).then_inc(M["act_rot"], 1)
                        elif what == "S":
                            r = it[1]
                            u, i, m, h = rows[r]
                            n = (i + 1) * P
                            c = {"a": 0, "c": 0, "sel": 2, "win": 4}[m] + h
                            act.wait_ge(M["dve_max"], r + 1)
                            if r >= NP_:
                                act.wait_ge(M["pe_t"], prob_of_row[r - NP_] + 1)
                            A(probs[:, r % NP_, 0:n], Sc[r % 2][:, 0:n], ACT.Exp, bias=nmax[:, r % 8:r % 8 + 1],
                              accum_out=sums[:, u % 2, i, c:c + 1]).then_inc(M["act_exp"], 1)
                        elif what == "T" and it[1] in pt_act.order:
                            copy_pt(act, it[1])
                        elif what == "cs":
                            act.wait_ge(M["cs_s"], it[1] - 3)
                            if it[1] > 4:
                                act.wait_ge(M["pe_misc"], misc.after(("ct", it[1] - 1)))
                            A(pc[:], cs_[:], ACT.Exp).then_inc(M["act_cx"], 1)
                        elif what == "SQ":
                            u, i = divmod(it[1], NQ)
                            act.wait_ge(M["dve_norm_o"], it[1] + 1)
                            A(sqj, y_q[:, i, :], ACT.Square, accum_out=msq[:, 0, i:i + 1]).then_inc(M["act_msq"], 1)
                            act.wait_ge(M["act_msq"], NQ * (u - 8) + i + 1)
                        elif what == "YS":
                            u = it[1]
                            act.wait_ge(M["dve_misc"], misc.after(("Y", u)))
                            if u >= 4:
                                act.wait_ge(M["pe_dense"], tile_of[(("bra", "brb")[u // 4 - 1], NM - 1)] + 1)
                            A(y_hi[:, u % 4, :], y_f[:, y_slot(u), :], ACT.Copy).then_inc(M["act_ys"], 1)

                    def merged_hi(m):
                        act.wait_ge(M["pe_dense"], T1 - 1)
                        act.wait_ge(M["dve_acc"], DA0 + m + 1)
                        A(h_hi[:, m, :], acc[:, m, :], ACT.Copy, scale=0.5).then_inc(M["act_merge"], 1)

                    def merge_tiles(i, m0, last):
                        for j in range(4):
                            t = T0 + 2 * m0 + j
                            if last and j == 3:
                                for m in range(EARLY):
                                    merged_hi(m)
                            hi(t + 2, i)
                            if j % 2 == 0:
                                act.wait_ge(M["pe_dense"], i * 4 + (t + 1))
                                act.wait_ge(M["dve_evac"], i * 2 + (DE0 + m0 + j // 2 - 1))
                                A(th[:, 1 - j // 2, :], Dn[t % 2][:], ACT.Tanh, scale=0.5).then_inc(M["act_evac"], 1)
                    with act.Fori(0, NM // 2 - 1) as i:
                        merge_tiles(i, 0, False)
                    merge_tiles(0, NM - 2, True)
                    for m in range(EARLY, NM):
                        merged_hi(m)
                    for c, b in ((0, Mb), (1, Ob)):
                        act.wait_ge(M["pe_p"], c + 1)
                        A(y_hi[:, c, :], b[:], ACT.Copy).then_inc(M["act_p"], 1)
                    with act.Fori(0, NM // 4) as i:
                        for j in range(4):
                            t = T1 + j
                            hi(t + 2, i)
                            act.wait_ge(M["dve_evac"], i * 4 + (DE1 + j + 1))
                            A(x1_hi[:, bass.ds(i * 4 + j, 1), :].rearrange("p a s -> p (a s)"),
                              xT[:, bass.ds(i * 4 + j, 1), :].rearrange("p a s -> p (a s)"), ACT.Copy).then_inc(M["act_x1"], 1)

                    def gate_tiles(i, m0, ahead):
                        for j in range(4):
                            t = T2 + 2 * m0 + j
                            if ahead or j < 2:
                                hi(t + 2, i, kt(("gate", "ple")[j % 2]), (0, 1) if j % 2 else (0,))
                            if j % 2 == 0:
                                act.wait_ge(M["pe_dense"], i * 4 + (t + 1))
                                act.wait_ge(M["dve_evac"], i * 2 + (DE2 + m0 + j // 2 - 1))
                                A(th[:, j // 2, :], Dn[t % 2][:], ACT.Tanh, scale=0.5).then_inc(M["act_evac"], 1)
                                if ahead or j < 2:
                                    hi(t + 2, i, kt("gate"), (1,))
                            else:
                                act.wait_ge(M["dve_x"], i * 2 + (m0 + j // 2 + 1))
                                act.wait_ge(M["pool_sum"], i * 2 + (m0 + j // 2 + 1))
                                A(probs[:, j // 2, :], xT[:, bass.ds(i * 2 + (m0 + j // 2), 1), :].rearrange("p a s -> p (a s)"),
                                  ACT.Square).then_inc(M["act_sq"], 1)
                    with act.Fori(0, NM // 2 - 1) as i:
                        gate_tiles(i, 0, True)
                    gate_tiles(0, NM - 2, False)

                @block.vector
                def _(dve):
                    chained = 0

                    def link(ins):
                        nonlocal chained
                        chained += 1
                        ins.then_inc(M["dve_chain"], 1)
                        dve.wait_ge(M["dve_chain"], chained)

                    TT, STT, TS, RED = dve.tensor_tensor, dve.scalar_tensor_tensor, dve.tensor_scalar, dve.tensor_reduce

                    def lo(t, i=None, k=8):
                        sl, n = t % SPL, (kt(kind_of(t)) if i is None else k) * P
                        for h, half in enumerate((slice(0, n // 2), slice(n // 2, n))):
                            dve.wait_ge(M["act_hi"], 2 * t + 1 + h if i is None else i * 8 + (2 * t + 1 + h))
                            TT(w_lo[:, sl, half], raw[:, t % RAW, half], f(w_hi[:, sl, half]), ALU.subtract).then_inc(M["dve_lo"], 1)

                    dve.wait_ge(M["pe_norm"], 1)
                    TS(rb[:], Mb[:], 1.0 / D, EPS, ALU.mult, ALU.add).then_inc(M["dve_norm"], 1)
                    dve.wait_ge(M["act_norm"], 2)
                    STT(rc[:], rs[:], -0.5, rs[:], ALU.mult, ALU.mult).then_inc(M["dve_norm"], 1)
                    dve.wait_ge(M["dve_norm"], 2)
                    TT(rc[:], rc[:], rb[:], ALU.mult).then_inc(M["dve_norm"], 1)
                    dve.wait_ge(M["pe_par"], 1)
                    dve.tensor_copy(par[:, 0:41], Ob[:, 0:41]).then_inc(M["dve_norm"], 1)
                    dve.wait_ge(M["dve_norm"], 4)
                    STT(rs[:], rc[:], 1.5, rs[:], ALU.add, ALU.mult).then_inc(M["dve_norm"], 1)
                    dve.wait_ge(M["dve_norm"], 5)
                    for m in range(NM):
                        if m >= 2:
                            dve.wait_ge(M["h_lo_s"], m - 1)
                        STT(th[:, m % 2, :], xT[:, m, :], par[:, m:m + 1], rs[:], ALU.mult, ALU.mult).then_inc(M["dve_norm"], 1)
                        if m == 0:
                            lo(0)
                        if m == NM // 2 + 1:
                            lo(1)
                    for it in items:
                        what = it[0]
                        if what == "end":
                            t = it[1]
                            kind, n, s = tiles[t]
                            Db = Dn[t % 2]
                            late_lo = evac_first(tiles, t)
                            if not late_lo:
                                lo(t + 2)
                            if kind in DVE_EVAC:
                                dve.wait_ge(M["pe_dense"], t + 1)
                                if kind in ACT_EVAC:
                                    dve.wait_ge(M["act_evac"], act_evac.after(t))
                            done = M["dve_evac"]
                            if kind == "fg":
                                dve.wait_ge(M["par2_ld"], 128)
                                TS(lf[:, 0, :], Db[0:8, :], bfor[:, 0:1], None, ALU.add).then_inc(done, 1)
                                dve.wait_ge(done, dve_evac.after(t))
                                link(TS(lf[:, 1, :], lf[:, 0, :], -1.0, None, ALU.mult))
                                TT(lf[:, 1, :], lf[:, 1, :], lf[:, 0, :], ALU.max).then_inc(M["lf_s"], 1)
                            elif kind in ("qa", "ka"):
                                src, dst = (q_hi, q_lo) if kind == "qa" else (k_hi, k_lo)
                                STT(dst[n % 2], Db[:], QSCALE if kind == "qa" else 1.0, f(src[n % 2]),
                                    ALU.mult, ALU.subtract).then_inc(done, 1)
                            elif kind in ("za", "zb", "zc"):
                                slot = th_slot[t]
                                STT(zs[:], th[:, slot, :], 1.0, Db[:], ALU.add, ALU.mult).then_inc(done, 1)
                            elif kind in ROTATED:
                                r = rots.after(t)
                                dve.wait_ge(M["act_evac"], act_evac.after(t))
                                if r > 1:
                                    dve.wait_ge(M["qk_s"], r - 1)
                                TT(rc[:], (qf if kind == "qb" else rx)[:], cosT[:], ALU.mult).then_inc(M["dve_rm"], 1)
                            elif kind in ("kcb", "vcb"):
                                if kind == "vcb":
                                    dve.wait_ge(M["flat_s"], 1)
                                else:
                                    dve.wait_ge(M["zero_s"], 1)
                                p0 = 8 if kind == "kcb" else 24
                                for g in range(2):
                                    tok = Db[HD * g:HD * g + HD, :].rearrange("p (c s) -> p s c", s=CS)
                                    for par_ in range(2):
                                        ps = slice(HD * par_, HD * par_ + HD)
                                        for mh in range(2):
                                            ins = TT(flat[ps, 8 * mh:8 * mh + 8, C32 * g:C32 * g + NC],
                                                     tok[:, par_:CS:2, mh:mh + NC],
                                                     par[ps, p0 + 8 * mh:p0 + 8 * mh + 8].unsqueeze(2).to_broadcast([HD, 8, NC]),
                                                     ALU.add)
                                ins.then_inc(done, 1)
                                dve.wait_ge(M["act_flat"], 1 if kind == "kcb" else 2)
                                TT(flat_lo, flat, f(flat_hi), ALU.subtract).then_inc(M["flat_s"], 1)
                            elif kind in ("w1k", "w1v"):
                                if n == 0 and kind == "w1v":
                                    dve.wait_ge(M["pe_misc"], misc.after(("ht", tile_of[("w1k", 3)])))
                                if n:
                                    dve.wait_ge(done, dve_evac.after(tile_of[(kind, n - 1)]))
                                TT(hacc, Db[0:2 * C32, 0:HIDDEN], b1[kind] if n == 0 else hacc, ALU.add).then_inc(done, 1)
                                if n == 3:
                                    dve.wait_ge(M["act_hid"], hids.after(kind))
                                    STT(hacc, hth, 1.0, hacc, ALU.add, ALU.mult).then_inc(M["dve_hid"], 1)
                            elif kind in ("bra", "brb"):
                                first = kind == "bra"
                                dst = acc[:, n, :] if first else rt[:]
                                dve.wait_ge(M["act_evac"], act_evac.after(tile_of[("mg" + kind[2], n)]))
                                STT(dst, th[:, th_slot[tile_of[("mg" + kind[2], n)]], :], 1.0, Db[:],
                                    ALU.add, ALU.mult).then_inc(done, 1)
                                if not first:
                                    dve.wait_ge(done, dve_evac.after(t))
                                    TT(acc[:, n, :], acc[:, n, :], rt[:], ALU.add).then_inc(M["dve_acc"], 1)
                            if late_lo:
                                lo(t + 2)
                        elif what == "lf2":
                            dve.wait_ge(M["act_lf"], 2)
                            link(TS(lf[:, 0, :], lf[:, 0, :], 0.0, None, ALU.min))
                            link(TS(lf[:, 2, :], lf[:, 0, :], 0.0, None, ALU.mult))
                            link(TT(lf[:, 0, :], lf[:, 0, :], lf[:, 3, :], ALU.subtract))
                            link(dve.tensor_tensor_scan(lf[:, 1, :], lf[:, 2, :], lf[:, 0, :], 0.0, ALU.add, ALU.add))
                            TS(ck[0:8, :], lf[:, 1, :], -1.0, None, ALU.mult).then_inc(M["ck_s"], 1)
                            dve.wait_ge(M["ck_s"], 1)
                            STT(ck[32:40, :], lf[:, 1, :], -1.0, f(ck[0:8, :]), ALU.mult, ALU.subtract).then_inc(M["ck_s"], 1)
                        elif what == "gates":
                            dve.wait_ge(M["pe_misc"], misc.after(it))
                            TS(gates[:], Mb[:].rearrange("p (i c) -> p i c", i=NQ)[:, :, 32:56], 0.5, 0.5,
                               ALU.mult, ALU.add).then_inc(M["dve_misc"], 1)
                            lv = lamr.rearrange("p (a two d) -> p a two d", a=2, two=2)
                            link(TT(tmp[:, 2 * P:3 * P].rearrange("p (a d) -> p a d", a=2), lv[:, :, 0, :], lv[:, :, 1, :], ALU.mult))
                            RED(lams[:, 0:2], tmp[:, 2 * P:3 * P].rearrange("p (a d) -> p a d", a=2), AX.X, ALU.add).then_inc(M["lam_s"], 1)
                            link(TT(gsc[:], par[:, 40:41], lconst[:, 1:2], ALU.mult))
                            dve.wait_ge(M["act_lam"], 1)
                            link(TT(lams[:, 4:5], lams[:, 3:4], lams[:, 2:3], ALU.subtract))
                            link(TT(lams[:, 5:6], lams[:, 4:5], lconst[:, 0:1], ALU.subtract))
                        elif what == "vt":
                            t = it[1]
                            kind, n, s = tiles[t]
                            dst = v_b[:, :, P * (kind == "vwb"):P * (kind == "vwb") + P] if kind[0:2] in ("vs", "vw") else v_ac[:, :, n * P:(n + 1) * P]
                            dve.wait_ge(M["pe_misc"], misc.after(it))
                            if kind == "vc" and n == 0:
                                dve.wait_ge(M["pe_v"], last_prob[(3, NQ - 1)] + 1)
                            dve.tensor_copy(dst, Mb[:].rearrange("p (i c) -> p i c", i=NQ)).then_inc(M["dve_misc"], 1)
                        elif what == "ht":
                            dve.wait_ge(M["pe_misc"], misc.after(it))
                            dve.tensor_copy(hid.rearrange("p a g b c -> p (a g) b c"),
                                            Mb[:, 0:4 * C32].rearrange("p (a c) -> p a c", c=C32).unsqueeze(2).to_broadcast(
                                                [P, 4, 4, C32])).then_inc(M["dve_misc"], 1)
                        elif what == "kcmp":
                            dve.wait_ge(M["pe_misc"], misc.after(it))
                            for g in range(2):
                                ps = slice(HD * g, HD * g + HD)
                                ins = TS(kcmpT[ps, C32 * g:C32 * g + C32], Mb[ps, C32 * g:C32 * g + C32], 0.5, None, ALU.mult)
                            ins.then_inc(M["dve_misc"], 1)
                        elif what == "vcmp":
                            dve.wait_ge(M["pe_misc"], misc.after(it))
                            for q in range(4):
                                ps, cs = slice(32 * q, 32 * q + 32), slice(HD * (q % 2), HD * (q % 2) + HD)
                                ins = TS(vbd[ps, cs], Mb[ps, cs], 0.5, None, ALU.mult)
                            ins.then_inc(M["dve_misc"], 1)
                        elif what == "rot":
                            t = it[1]
                            hi_, lo_, u = rot_dst(*tiles[t][:2])
                            r = rots.after(t)
                            dve.wait_ge(M["pool_rot"], r)
                            dve.wait_ge(M["dve_rm"], r)
                            TT(rc[:], rc[:], rb[:], ALU.add).then_inc(M["dve_rs"], 1)
                            dve.wait_ge(M["act_rot"], r)
                            TT(lo_, rc[:], f(hi_), ALU.subtract).then_inc(M["qk_s"], 1)
                        elif what == "S":
                            r = it[1]
                            n = (rows[r][1] + 1) * P
                            dve.wait_ge(M["pe_s"], r + 1)
                            if r >= 8:
                                dve.wait_ge(M["act_exp"], r - 7)
                            RED(nmax[:, r % 8:r % 8 + 1], Sc[r % 2][:, 0:n], AX.X, ALU.max, negate=True).then_inc(M["dve_max"], 1)
                        elif what == "T" and it[1] in pt_dve.order:
                            copy_pt(dve, it[1])
                        elif what == "CB":
                            r = it[1]
                            u, i, _, _ = rows[r]
                            n, b = (i + 1) * P, u % 2
                            p0, p1 = probs[:, (r - 1) % NP_, 0:n], probs[:, r % NP_, 0:n]
                            dve.wait_ge(M["act_exp"], r + 1)
                            link(dve.reciprocal(coef[:, b, 0:2], sums[:, b, i, 0:2]))
                            link(TT(coef[:, b, 2:3], coef[:, b, 1:2], lams[:, 5:6], ALU.mult))
                            link(TS(p0, p0, coef[:, b, 0:1], None, ALU.mult))
                            STT(p0, p1, coef[:, b, 2:3], p0, ALU.mult, ALU.add).then_inc(M["dve_comb"], 1)
                        elif what == "cs":
                            u = it[1]
                            dve.wait_ge(M["pe_misc"], misc.after(it))
                            if u > 4:
                                dve.wait_ge(M["act_cx"], u - 4)
                            TT(cs_[:], Mb[:, 0:2 * NQ * C32].rearrange("p (i h c) -> p i h c", i=NQ, h=2),
                               cmask[:].unsqueeze(2).to_broadcast([P, NQ, 2, C32]), ALU.add).then_inc(M["dve_misc"], 1)
                            dve.wait_ge(M["dve_misc"], misc.after(it))
                            link(RED(cmx[:], cs_[:].rearrange("p i h c -> p (i h) c"), AX.X, ALU.max))
                            TT(cs_[:].rearrange("p i h c -> p (i h) c"), cs_[:].rearrange("p i h c -> p (i h) c"),
                               cmx[:].unsqueeze(2).to_broadcast([P, 2 * NQ, C32]), ALU.subtract).then_inc(M["cs_s"], 1)
                        elif what == "cx":
                            u = it[1]
                            dve.wait_ge(M["act_cx"], u - 3)
                            link(RED(sums[:, u % 2, :, 0:2], pc[:], AX.X, ALU.add))
                            for h in range(2):
                                ins = STT(pc[:, :, h, :], cmask[:], 0.0, pc[:, :, h, :], ALU.is_equal, ALU.mult)
                            ins.then_inc(M["cprob_s"], 1)
                        elif what == "ct":
                            u = it[1]
                            dve.wait_ge(M["pe_misc"], misc.after(it))
                            if u > 4:
                                dve.wait_ge(M["pe_v"], last_prob[(u - 1, NQ - 1)] + 1)
                            dve.tensor_copy(pcT[:], Mb[:, 0:2 * P].rearrange("p (g q) -> p g q", g=2)).then_inc(M["dve_misc"], 1)
                        elif what == "N":
                            u, i = divmod(it[1], NQ)
                            b = u % 2
                            dve.wait_ge(M["pe_v"], last_prob[(u, i)] + 1)
                            if u and i == 0:
                                dve.wait_ge(M["pe_misc"], misc.after(("Y", u - 1)))
                            if branch(u) == "A":
                                link(dve.reciprocal(coef[:, b, 0:2], sums[:, b, i, 0:2]))
                                TT(y_q[:, i, :].rearrange("p (h d) -> p h d", h=2), Ob[:, 0:P].rearrange("p (h d) -> p h d", h=2),
                                   coef[:, b, 0:2].unsqueeze(2).to_broadcast([P, 2, HD]), ALU.mult).then_inc(M["dve_norm_o"], 1)
                            elif branch(u) == "B":
                                link(dve.reciprocal(coef[:, b, 0:6], sums[:, b, i, 0:6]))
                                gv = gates[:, i, :].rearrange("p (g n b) -> p b g n", g=2, n=4)[:, :, :, u - 4]
                                link(TT(coef[:, b, 0:6].rearrange("p (b h) -> p b h", b=3),
                                        coef[:, b, 0:6].rearrange("p (b h) -> p b h", b=3), gv, ALU.mult))
                                TT(tmp[:].rearrange("p (b d) -> p b d", b=6), Ob[:, 0:384].rearrange("p (b d) -> p b d", b=6),
                                   coef[:, b, 0:6].unsqueeze(2).to_broadcast([P, 6, HD]), ALU.mult).then_inc(M["dve_norm_o"], 1)
                                dve.wait_ge(M["dve_norm_o"], it[1] + 1)
                                RED(y_q[:, i, :], tmp[:].rearrange("p (b f) -> p f b", b=3), AX.X, ALU.add).then_inc(M["yq_s"], 1)
                                dve.wait_ge(M["yq_s"], it[1] + 1 - 4 * NQ)
                            else:
                                dve.tensor_copy(y_q[:, i, :], Ob[:, 0:P]).then_inc(M["dve_norm_o"], 1)
                        elif what == "MS":
                            u = it[1]
                            dve.wait_ge(M["act_msq"], NQ * (u - 7))
                            TS(msq[:, 1, :], msq[:, 0, :], 1.0 / P, EPS, ALU.mult, ALU.add).then_inc(M["ms_s"], 1)
                        elif what == "YN":
                            u = it[1]
                            dve.wait_ge(M["pool_pow"], u - 7)
                            link(TT(msq[:, 3, :], msq[:, 2, :], msq[:, 2, :], ALU.mult))
                            link(TT(msq[:, 3, :], msq[:, 3, :], msq[:, 1, :], ALU.mult))
                            link(TS(msq[:, 3, :], msq[:, 3, :], -0.5, 1.5, ALU.mult, ALU.add))
                            link(TT(msq[:, 3, :], msq[:, 3, :], msq[:, 2, :], ALU.mult))
                            TT(y_q[:], y_q[:], msq[:, 3, :].unsqueeze(2).to_broadcast([P, NQ, P]),
                               ALU.mult).then_inc(M["yqc_s"], 1)
                        elif what == "Y":
                            u = it[1]
                            dve.wait_ge(M["pe_misc"], misc.after(it))
                            if u >= 4:
                                dve.wait_ge(M["dve_ysplit"], ysplit.after(u - 4))
                            z = tile_of[("z" + branch(u).lower(), u % 4)]
                            dve.wait_ge(M["dve_evac"], dve_evac.after(z))
                            STT(y_f[:, y_slot(u), :], Mb[:], gsc[:, 0:1] if branch(u) == "C" else 0.5, zs[:],
                                ALU.mult, ALU.mult).then_inc(M["dve_misc"], 1)
                        elif what == "YS":
                            u = it[1]
                            dve.wait_ge(M["act_ys"], ysplit.after(u))
                            TT(y_lo[:, u % 4, :], y_f[:, y_slot(u), :], f(y_hi[:, u % 4, :]), ALU.subtract).then_inc(M["dve_ysplit"], 1)

                    def merged_lo(m):
                        dve.wait_ge(M["act_merge"], m + 1)
                        STT(h_lo[:, m, :], acc[:, m, :], 0.5, f(h_hi[:, m, :]), ALU.mult, ALU.subtract).then_inc(M["dve_merge"], 1)

                    def merge_tiles(i, m0, last):
                        for j in range(4):
                            t = T0 + 2 * m0 + j
                            if last and j == 3:
                                for m in range(EARLY):
                                    merged_lo(m)
                            lo(t + 2, i)
                            if j % 2:
                                dve.wait_ge(M["act_evac"], i * 2 + (AE0 + m0 + j // 2 + 1))
                                dve.wait_ge(M["pe_dense"], i * 4 + (t + 1))
                                dve.wait_ge(M["dve_acc"], i * 2 + (DA0 + m0 + j // 2))
                                STT(rt[:], th[:, 1 - j // 2, :], 1.0, Dn[t % 2][:], ALU.add, ALU.mult).then_inc(M["dve_evac"], 1)
                                dve.wait_ge(M["dve_evac"], i * 2 + (DE0 + m0 + j // 2 + 1))
                                am = acc[:, bass.ds(i * 2 + (m0 + j // 2), 1), :].rearrange("p a s -> p (a s)")
                                TT(am, am, rt[:], ALU.add).then_inc(M["dve_acc"], 1)
                    with dve.Fori(0, NM // 2 - 1) as i:
                        merge_tiles(i, 0, False)
                    merge_tiles(0, NM - 2, True)
                    for m in range(EARLY, NM):
                        merged_lo(m)
                    for c, b in ((0, Mb), (1, Ob)):
                        dve.wait_ge(M["act_p"], c + 1)
                        TT(y_lo[:, c, :], b[:], f(y_hi[:, c, :]), ALU.subtract).then_inc(M["dve_p"], 1)
                    with dve.Fori(0, NM // 4) as i:
                        for j in range(4):
                            t = T1 + j
                            xm = xT[:, bass.ds(i * 4 + j, 1), :].rearrange("p a s -> p (a s)")
                            lo(t + 2, i)
                            dve.wait_ge(M["pe_dense"], i * 4 + (t + 1))
                            TT(xm, Dn[t % 2][:], xm, ALU.add).then_inc(M["dve_evac"], 1)
                            dve.wait_ge(M["act_x1"], i * 4 + (j + 1))
                            TT(x1_lo[:, bass.ds(i * 4 + j, 1), :].rearrange("p a s -> p (a s)"), xm,
                               f(x1_hi)[:, bass.ds(i * 4 + j, 1), :].rearrange("p a s -> p (a s)"),
                               ALU.subtract).then_inc(M["x1_s"], 1)

                    def gate_tiles(i, m0, ahead):
                        for j in range(4):
                            t = T2 + 2 * m0 + j
                            if ahead or j < 2:
                                lo(t + 2, i, kt(("gate", "ple")[j % 2]))
                            if j % 2:
                                xm = xT[:, bass.ds(i * 2 + (m0 + j // 2), 1), :].rearrange("p a s -> p (a s)")
                                dve.wait_ge(M["act_evac"], i * 2 + (AE1 + m0 + j // 2 + 1))
                                dve.wait_ge(M["pe_dense"], i * 4 + (t + 1))
                                STT(rt[:], th[:, j // 2, :], 1.0, Dn[t % 2][:], ALU.add, ALU.mult).then_inc(M["dve_evac"], 1)
                                dve.wait_ge(M["dve_evac"], i * 2 + (DE2 + m0 + j // 2 + 1))
                                STT(xm, rt[:], 0.5, xm, ALU.mult, ALU.add).then_inc(M["dve_x"], 1)
                    with dve.Fori(0, NM // 2 - 1) as i:
                        gate_tiles(i, 0, True)
                    gate_tiles(0, NM - 2, False)

            nc.gpsimd.sem_clear(range(layer_sems[0].num, layer_sems[-1].num + 1))
            nc.all_engine_barrier()

        o_pe, o_act, o_dve, o_t, o_c, o_st = (sem(n) for n in ("o_pe", "o_act", "o_dve", "o_t", "o_c", "o_st"))
        with nc.Block() as block:
            @block.tensor
            def _(pe):
                pe.matmul(Mb[:], ones[:], ssum[:], start=True, stop=True).then_inc(o_pe, 1)
                for m in range(NM):
                    pe.wait_ge(o_dve, 4 + m + 1)
                    if m >= 2:
                        pe.wait_ge(o_c, m - 1)
                    for i in range(NQ):
                        ins = pe.transpose(Dn[m % 2][:, i * P:(i + 1) * P], th[:, m % 2, i * P:(i + 1) * P], ident[:])
                    ins.then_inc(o_t, 1)

            @block.scalar
            def _(act):
                act.wait_ge(o_dve, 1)
                act.activation(rx[:], rb[:], ACT.Ln).then_inc(o_act, 1)
                act.wait_ge(o_act, 1)
                act.activation(rs[:], rx[:], ACT.Exp, scale=-0.5).then_inc(o_act, 1)
                for m in range(NM):
                    act.wait_ge(o_t, m + 1)
                    act.activation(x_tok[:, :, m * P:(m + 1) * P], Dn[m % 2][:].rearrange("p (i c) -> p i c", i=NQ),
                                   ACT.Copy).then_inc(o_c, 1)

            @block.vector
            def _(dve):
                dve.wait_ge(o_pe, 1)
                dve.tensor_scalar(rb[:], Mb[:], 1.0 / D, EPS, ALU.mult, ALU.add).then_inc(o_dve, 1)
                dve.wait_ge(o_act, 2)
                dve.scalar_tensor_tensor(rc[:], rs[:], -0.5, rs[:], ALU.mult, ALU.mult).then_inc(o_dve, 1)
                dve.wait_ge(o_dve, 2)
                dve.tensor_tensor(rc[:], rc[:], rb[:], ALU.mult).then_inc(o_dve, 1)
                dve.wait_ge(o_dve, 3)
                dve.scalar_tensor_tensor(rs[:], rc[:], 1.5, rs[:], ALU.add, ALU.mult).then_inc(o_dve, 1)
                dve.wait_ge(o_dve, 4)
                for m in range(NM):
                    if m >= 2:
                        dve.wait_ge(o_t, m - 1)
                    dve.scalar_tensor_tensor(th[:, m % 2, :], xT[:, m, :], finp[:, m:m + 1], rs[:],
                                             ALU.mult, ALU.mult).then_inc(o_dve, 1)

            @block.sync
            def _(sp):
                half = NM // 2
                for c in range(2):
                    sp.wait_ge(o_c, half * (c + 1))
                    cols = slice(c * half * P, (c + 1) * half * P)
                    sp.dma_start(out.rearrange("a (t p) d -> p (a t) d", p=P)[:, :, cols], x_tok[:, :, cols]).then_inc(o_st, 16)
                sp.wait_ge(o_st, 32)


_INS = ["x", "p", "positions", "norm_g", "w_in", "b_forget", "cmp_pe_k", "cmp_w1_k", "cmp_b1_k", "cmp_w2_k",
        "cmp_pe_v", "cmp_w1_v", "cmp_b1_v", "cmp_w2_v", "diff_lam", "diff_subln_g",
        "w_br_a", "w_br_b", "w_br_c", "w_out", "w_ple", "w_ple_gate", "final_g"]


def kernel(**inputs):
    import numpy as _np
    import concourse.bacc as _bacc
    from concourse import mybir as _mybir
    from concourse.bass_utils import run_bass_kernel_spmd as _run

    nc = _bacc.Bacc("TRN2", target_bir_lowering=False, num_devices=1)
    depth = inputs["norm_g"].shape[0]
    half = HD // 2
    freq = _np.float32(ROPE_THETA) ** (-_np.arange(half, dtype=_np.float32) / _np.float32(half))
    rope_consts = _np.stack([_np.tile(freq, P // half), _np.tile(_np.repeat([-1.0, 1.0], half), P // HD)], 1)
    lam0 = _np.array([0.8 - 0.6 * _np.exp(-0.3 * i) for i in range(depth)])
    layer_consts = _np.tile(_np.stack([lam0, 0.5 * (1.0 - lam0)], 1)[:, None, :], (1, P, 1))
    arrays, args = {}, []
    for name in _INS + ["rope_consts", "layer_consts"]:
        a = {"rope_consts": rope_consts, "layer_consts": layer_consts}.get(name)
        a = _np.ascontiguousarray(inputs[name] if a is None else a.astype(_np.float32))
        arrays[f"in_{name}_dram"] = a
        args.append(nc.dram_tensor(f"in_{name}_dram", a.shape, _mybir.dt.from_np(a.dtype), kind="ExternalInput").ap())
    args.append(nc.dram_tensor("out_dram", inputs["x"].shape, F32, kind="ExternalOutput").ap())
    hybrid_trunk(nc, *args)
    r = _run(nc, [arrays], core_ids=[0])
    return r.results[0]["out_dram"]
```
